# Optimizing a Trainium2 kernel written in Bass

```python
import math
import jax, jax.numpy as jnp
from jax import lax
import numpy as np

D_MODEL = 2048
BATCH = 1
SEQ = 256
DEPTH = 1

HEAD_DIM = 128
MIX_WIDTH = D_MODEL
A_HEADS = MIX_WIDTH // (2 * HEAD_DIM)
B_HEADS = MIX_WIDTH // (2 * HEAD_DIM)
A_WIDTH = A_HEADS * HEAD_DIM
B_WIDTH = B_HEADS * HEAD_DIM
DIFF_DIM = HEAD_DIM // 2
IN_WIDTH = 3 * A_WIDTH + 3 * B_WIDTH
DILATED_CONFIGS = ((128, 1), (512, 4), (2048, 16))
ROPE_THETA = 500000.0
ROPE_FRACTION = 4
D_FF = ((-(-8 * D_MODEL // 3) + 255) // 256) * 256
Q_BLOCK = 128
RMS_EPS = 1e-6
SUBLN_EPS = 1e-5
NEG_INF = -1e30


def rmsnorm(x, g, eps=RMS_EPS):
    xf = x.astype(jnp.float32)
    y = xf * lax.rsqrt(jnp.mean(xf * xf, axis=-1, keepdims=True) + eps)
    return (y * g.astype(jnp.float32)).astype(x.dtype)

def rope_tables(seq, rot_dim):
    inv_freq = ROPE_THETA ** (-jnp.arange(0, rot_dim, 2, dtype=jnp.float32) / rot_dim)
    ang = jnp.arange(seq, dtype=jnp.float32)[:, None] * inv_freq[None, :]
    return jnp.cos(ang), jnp.sin(ang)

def rope(x, cos, sin):
    r2 = cos.shape[-1]
    shape = (x.shape[1],) + (1,) * (x.ndim - 3) + (r2,)
    c, s = cos.reshape(shape), sin.reshape(shape)
    x1, x2 = x[..., :r2], x[..., r2:2 * r2]
    return jnp.concatenate([x1 * c - x2 * s, x2 * c + x1 * s, x[..., 2 * r2:]], axis=-1).astype(x.dtype)

def dilated_branch(q, k, v, dil, half):
    B, S, H, Dh = q.shape
    L = S // dil
    nb = -(-L // half)
    Lp = nb * half

    def by_residue(a):
        return a.reshape(B, L, dil, H, Dh).transpose(0, 2, 3, 1, 4)

    qs = jnp.pad(by_residue(q), ((0, 0), (0, 0), (0, 0), (0, Lp - L), (0, 0))).reshape(B, dil, H, nb, half, Dh)
    kpad = ((0, 0), (0, 0), (0, 0), (half, Lp - L + half), (0, 0))
    kp = jnp.pad(by_residue(k), kpad).reshape(B, dil, H, nb + 2, half, Dh)
    vp = jnp.pad(by_residue(v), kpad).reshape(B, dil, H, nb + 2, half, Dh)

    def band(a):
        return jnp.concatenate([a[:, :, :, :-2], a[:, :, :, 1:-1], a[:, :, :, 2:]], axis=4)

    kb, vb = band(kp), band(vp)
    s = jnp.einsum('brhnqe,brhnke->brhnqk', qs, kb, preferred_element_type=jnp.float32) * (Dh ** -0.5)
    blk = jnp.arange(nb)[:, None, None]
    qa = jnp.arange(half)[None, :, None]
    kj = jnp.arange(3 * half)[None, None, :]
    kpos = blk * half - half + kj
    dist = kj - half - qa
    mask = (jnp.abs(dist) <= half) & (kpos >= 0) & (kpos < L)
    s = jnp.where(mask, s, NEG_INF)
    m = jnp.max(s, axis=-1, keepdims=True)
    p = jnp.exp(s - m)
    den = jnp.sum(p, axis=-1)
    o = jnp.einsum('brhnqk,brhnke->brhnqe', p, vb.astype(jnp.float32)) / den[..., None]
    lse = m[..., 0] + jnp.log(den)
    o = o.reshape(B, dil, H, Lp, Dh)[:, :, :, :L].transpose(0, 3, 1, 2, 4).reshape(B, S, H, Dh)
    lse = lse.reshape(B, dil, H, Lp)[:, :, :, :L].transpose(0, 3, 1, 2).reshape(B, S, H)
    return o, lse

def dilated_attention(q, k, v):
    outs, lses = [], []
    for window, dil in DILATED_CONFIGS:
        o, lse = dilated_branch(q, k, v, dil, window // (2 * dil))
        outs.append(o)
        lses.append(lse)
    w = jax.nn.softmax(jnp.stack(lses, axis=0), axis=0)
    return jnp.einsum('gbsh,gbshe->bshe', w, jnp.stack(outs, axis=0))

def diff_attention(q, k, v, lam):
    B, S, H, _, d = q.shape
    nqb = S // Q_BLOCK
    qb = q.reshape(B, nqb, Q_BLOCK, H, 2, d).transpose(1, 0, 3, 4, 2, 5)
    kt = k.transpose(0, 2, 3, 1, 4)
    vt = v.transpose(0, 2, 1, 3)

    def one_block(qblk):
        s = jnp.einsum('bhcqe,bhcke->bhcqk', qblk, kt, preferred_element_type=jnp.float32) * (d ** -0.5)
        p = jax.nn.softmax(s, axis=-1)
        a = p[:, :, 0] - lam * p[:, :, 1]
        return jnp.einsum('bhqk,bhke->bhqe', a, vt.astype(jnp.float32))

    o = lax.map(one_block, qb)
    return o.transpose(1, 0, 3, 2, 4).reshape(B, S, H, 2 * d)

def first_inputs(seed: int = 0) -> dict:
    key = jax.random.key(seed)
    ks = jax.random.split(key, 11)
    f32 = jnp.float32

    def dense(k, shape):
        return jax.random.normal(k, shape, f32) * (shape[-2] ** -0.5)

    def gain(k, shape):
        return 1.0 + 0.02 * jax.random.normal(k, shape, f32)

    return {
        'x': jax.random.normal(ks[0], (BATCH, SEQ, D_MODEL), f32),
        'norm_attn': gain(ks[1], (DEPTH, D_MODEL)),
        'w_in': dense(ks[2], (DEPTH, D_MODEL, IN_WIDTH)),
        'lambda_qk': 0.1 * jax.random.normal(ks[3], (DEPTH, 4, DIFF_DIM), f32),
        'subln': gain(ks[4], (DEPTH, 2 * DIFF_DIM)),
        'w_out': dense(ks[5], (DEPTH, MIX_WIDTH, D_MODEL)),
        'norm_ffn': gain(ks[6], (DEPTH, D_MODEL)),
        'w_gate': dense(ks[7], (DEPTH, D_MODEL, D_FF)),
        'w_up': dense(ks[8], (DEPTH, D_MODEL, D_FF)),
        'w_down': dense(ks[9], (DEPTH, D_FF, D_MODEL)),
        'norm_final': gain(ks[10], (D_MODEL,)),
    }

def first_block(x, norm_attn, w_in, lambda_qk, subln, w_out, norm_ffn, w_gate, w_up, w_down, norm_final):
    B, S, _ = x.shape
    cos_a, sin_a = rope_tables(S, HEAD_DIM // ROPE_FRACTION)
    cos_b, sin_b = rope_tables(S, DIFF_DIM // ROPE_FRACTION)
    splits = [A_WIDTH, 2 * A_WIDTH, 3 * A_WIDTH, 3 * A_WIDTH + B_WIDTH, 3 * A_WIDTH + 2 * B_WIDTH]
    for l in range(DEPTH):
        h = rmsnorm(x, norm_attn[l])
        proj = h @ w_in[l]
        qa, ka, va, qb, kb, vb = jnp.split(proj, splits, axis=-1)
        qa = rope(qa.reshape(B, S, A_HEADS, HEAD_DIM), cos_a, sin_a)
        ka = rope(ka.reshape(B, S, A_HEADS, HEAD_DIM), cos_a, sin_a)
        va = va.reshape(B, S, A_HEADS, HEAD_DIM)
        ya = dilated_attention(qa, ka, va).astype(x.dtype).reshape(B, S, A_WIDTH)
        lam_init = 0.8 - 0.6 * math.exp(-0.3 * l)
        lq = lambda_qk[l].astype(jnp.float32)
        lam = jnp.exp(jnp.sum(lq[0] * lq[1])) - jnp.exp(jnp.sum(lq[2] * lq[3])) + lam_init
        qb = rope(qb.reshape(B, S, B_HEADS, 2, DIFF_DIM), cos_b, sin_b)
        kb = rope(kb.reshape(B, S, B_HEADS, 2, DIFF_DIM), cos_b, sin_b)
        vb = vb.reshape(B, S, B_HEADS, 2 * DIFF_DIM)
        yb = diff_attention(qb, kb, vb, lam)
        yb = (rmsnorm(yb, subln[l], SUBLN_EPS) * (1.0 - lam_init)).astype(x.dtype).reshape(B, S, B_WIDTH)
        x = x + jnp.concatenate([ya, yb], axis=-1) @ w_out[l]
        h = rmsnorm(x, norm_ffn[l])
        x = x + (jax.nn.silu(h @ w_gate[l]) * (h @ w_up[l])) @ w_down[l]
    return rmsnorm(x, norm_final)


RET_HEADS = 4
RET_HEAD_DIM = 256
RET_WIDTH = RET_HEADS * RET_HEAD_DIM
RET_CHUNK = 128
RET_ROPE_THETA = 10000.0
MOBA_HEADS = 8
MOBA_HEAD_DIM = 128
MOBA_WIDTH = MOBA_HEADS * MOBA_HEAD_DIM
MOBA_BLOCK = 256
MOBA_TOPK = 3
MOBA_Q_CHUNK = 64
ROT_DIM = MOBA_HEAD_DIM // 4
D_FF_2 = 5632
CONV_WIDTH = 3
EPS = 1e-6
IN_SIZES = (RET_WIDTH, RET_WIDTH, RET_WIDTH, RET_WIDTH,
            MOBA_WIDTH, MOBA_WIDTH, MOBA_WIDTH,
            D_MODEL, D_MODEL)
IN_TOTAL = sum(IN_SIZES)


def rmsnorm_2(x, w):
    xf = x.astype(jnp.float32)
    y = xf * lax.rsqrt(jnp.mean(xf * xf, axis=-1, keepdims=True) + EPS)
    return (y * w.astype(jnp.float32)).astype(x.dtype)

def rotary(x, rot_dim, theta):
    S = x.shape[1]
    pos = jnp.arange(S, dtype=jnp.float32)
    inv_freq = jnp.asarray(theta, jnp.float32) ** (-jnp.arange(0, rot_dim, 2, dtype=jnp.float32) / rot_dim)
    ang = pos[:, None] * inv_freq[None, :]
    cos = jnp.cos(ang)[None, :, None, :]
    sin = jnp.sin(ang)[None, :, None, :]
    xr = x[..., :rot_dim].astype(jnp.float32)
    x1, x2 = jnp.split(xr, 2, axis=-1)
    rot = jnp.concatenate([x1 * cos - x2 * sin, x2 * cos + x1 * sin], axis=-1).astype(x.dtype)
    return jnp.concatenate([rot, x[..., rot_dim:]], axis=-1)

def retention(q, k, v):
    B, S, H, dk = q.shape
    dv = v.shape[-1]
    C = RET_CHUNK
    N = S // C
    q = q.astype(jnp.float32)
    k = k.astype(jnp.float32) * (dk ** -0.5)
    v = v.astype(jnp.float32)
    log_g = jnp.log1p(-jnp.exp2(-5.0 - jnp.arange(H, dtype=jnp.float32)))
    i = jnp.arange(C, dtype=jnp.float32)
    diff = i[:, None] - i[None, :]
    causal = diff >= 0
    decay = jnp.where(causal[None], jnp.exp(log_g[:, None, None] * jnp.where(causal, diff, 0.0)[None]), 0.0)
    xi = jnp.exp(log_g[:, None] * (i[None, :] + 1.0))
    zeta = jnp.exp(log_g[:, None] * (C - 1.0 - i[None, :]))
    g_chunk = jnp.exp(log_g * C)

    def to_chunks(t):
        return t.reshape(B, N, C, H, t.shape[-1]).transpose(1, 0, 3, 2, 4)

    def step(state, xs):
        qc, kc, vc = xs
        scores = jnp.einsum('bhqd,bhkd->bhqk', qc, kc) * decay[None]
        inner = jnp.einsum('bhqk,bhkd->bhqd', scores, vc)
        cross = jnp.einsum('bhqd,bhde->bhqe', qc, state) * xi[None, :, :, None]
        new_state = state * g_chunk[None, :, None, None] + jnp.einsum(
            'bhkd,bhke->bhde', kc * zeta[None, :, :, None], vc)
        return new_state, inner + cross

    init = jnp.zeros((B, H, dk, dv), jnp.float32)
    _, out = lax.scan(step, init, (to_chunks(q), to_chunks(k), to_chunks(v)))
    return out.transpose(1, 0, 3, 2, 4).reshape(B, S, H, dv)

def moba_attention(q, k, v):
    B, S, H, d = q.shape
    dtype = q.dtype
    BS = MOBA_BLOCK
    Cq = MOBA_Q_CHUNK
    NB = -(-S // BS)
    S_pad = NB * BS
    NQ = S // Cq
    topk = min(MOBA_TOPK, NB)
    scale = d ** -0.5
    qh = q.transpose(0, 2, 1, 3)
    pad = ((0, 0), (0, 0), (0, S_pad - S), (0, 0))
    kb = jnp.pad(k.transpose(0, 2, 1, 3), pad).reshape(B, H, NB, BS, d)
    vb = jnp.pad(v.transpose(0, 2, 1, 3), pad).reshape(B, H, NB, BS, d)
    kmean = jnp.mean(kb.astype(jnp.float32), axis=3)
    q_all = qh.reshape(B, H, NQ, Cq, d).transpose(0, 2, 1, 3, 4).reshape(B * NQ, H, Cq, d)
    b_idx = jnp.repeat(jnp.arange(B, dtype=jnp.int32), NQ)
    n_idx = jnp.tile(jnp.arange(NQ, dtype=jnp.int32), B)
    hh = jnp.arange(H)[:, None, None]

    def step(args):
        qc, b, n = args
        kb_b, vb_b, km_b = kb[b], vb[b], kmean[b]
        q0 = n * Cq
        cb = q0 // BS
        qpos = q0 + jnp.arange(Cq)
        bscore = jnp.einsum('hqd,hnd->hqn', qc.astype(jnp.float32), km_b)
        past = jnp.arange(NB) < cb
        bscore = jnp.where(past[None, None, :], bscore, -jnp.inf)
        _, idx = lax.top_k(bscore, topk)
        valid = idx < cb
        k_sel = kb_b[hh, idx]
        v_sel = vb_b[hh, idx]
        s_sel = jnp.einsum('hqd,hqnkd->hqnk', qc, k_sel, preferred_element_type=jnp.float32) * scale
        s_sel = jnp.where(valid[..., None], s_sel, -jnp.inf).reshape(H, Cq, topk * BS)
        k_own = lax.dynamic_index_in_dim(kb_b, cb, axis=1, keepdims=False)
        v_own = lax.dynamic_index_in_dim(vb_b, cb, axis=1, keepdims=False)
        s_own = jnp.einsum('hqd,hkd->hqk', qc, k_own, preferred_element_type=jnp.float32) * scale
        kpos = cb * BS + jnp.arange(BS)
        s_own = jnp.where((kpos[None, :] <= qpos[:, None])[None], s_own, -jnp.inf)
        p = jax.nn.softmax(jnp.concatenate([s_sel, s_own], axis=-1), axis=-1).astype(dtype)
        p_sel = p[..., :topk * BS].reshape(H, Cq, topk, BS)
        p_own = p[..., topk * BS:]
        o = jnp.einsum('hqnk,hqnkd->hqd', p_sel, v_sel) + jnp.einsum('hqk,hkd->hqd', p_own, v_own)
        return o.astype(dtype)

    out = lax.map(step, (q_all, b_idx, n_idx))
    return out.reshape(B, NQ, H, Cq, d).transpose(0, 1, 3, 2, 4).reshape(B, S, H * d)

def causal_dwconv(u, w, b):
    S = u.shape[1]
    up = jnp.pad(u, ((0, 0), (CONV_WIDTH - 1, 0), (0, 0)))
    y = b
    for j in range(CONV_WIDTH):
        y = y + w[j] * up[:, j:j + S]
    return y

def second_inputs(seed: int = 0) -> dict:
    key = jax.random.key(seed)
    ks = jax.random.split(key, 14)
    f32 = jnp.float32

    def normal(k, shape, scale):
        return jax.random.normal(k, shape, f32) * scale

    def gain(k, shape):
        return 1.0 + 0.05 * jax.random.normal(k, shape, f32)

    return {
        "x": jax.random.normal(ks[0], (BATCH, SEQ, D_MODEL), f32),
        "attn_norm_w": gain(ks[1], (DEPTH, D_MODEL)),
        "w_in": normal(ks[2], (DEPTH, D_MODEL, IN_TOTAL), D_MODEL ** -0.5),
        "ret_norm_w": gain(ks[3], (DEPTH, RET_WIDTH)),
        "w_ret_up": normal(ks[4], (DEPTH, RET_WIDTH, D_MODEL), RET_WIDTH ** -0.5),
        "w_moba_up": normal(ks[5], (DEPTH, MOBA_WIDTH, D_MODEL), MOBA_WIDTH ** -0.5),
        "w_out": normal(ks[6], (DEPTH, D_MODEL, D_MODEL), D_MODEL ** -0.5),
        "ffn_norm_w": gain(ks[7], (DEPTH, D_MODEL)),
        "w_ffn_up": normal(ks[8], (DEPTH, D_MODEL, 2 * D_FF_2), D_MODEL ** -0.5),
        "conv_w": normal(ks[9], (DEPTH, CONV_WIDTH, 2 * D_FF_2), CONV_WIDTH ** -0.5),
        "conv_b": normal(ks[10], (DEPTH, 2 * D_FF_2), 0.01),
        "w_ffn_down": normal(ks[11], (DEPTH, D_FF_2, D_MODEL), D_FF_2 ** -0.5),
        "final_norm_w": gain(ks[12], (D_MODEL,)),
    }

def second_block(x, attn_norm_w, w_in, ret_norm_w, w_ret_up, w_moba_up, w_out,
              ffn_norm_w, w_ffn_up, conv_w, conv_b, w_ffn_down, final_norm_w):
    B, S, _ = x.shape
    split_at = [int(s) for s in np.cumsum(IN_SIZES)[:-1]]
    for l in range(DEPTH):
        h = rmsnorm_2(x, attn_norm_w[l])
        proj = h @ w_in[l]
        rq, rk, rv, rg, mq, mk, mv, g_ret, g_moba = jnp.split(proj, split_at, axis=-1)
        rq = rotary(rq.reshape(B, S, RET_HEADS, RET_HEAD_DIM), RET_HEAD_DIM, RET_ROPE_THETA)
        rk = rotary(rk.reshape(B, S, RET_HEADS, RET_HEAD_DIM), RET_HEAD_DIM, RET_ROPE_THETA)
        rv = rv.reshape(B, S, RET_HEADS, RET_HEAD_DIM)
        o_ret = retention(rq, rk, rv)
        o_ret = o_ret * lax.rsqrt(jnp.mean(o_ret * o_ret, axis=-1, keepdims=True) + EPS)
        o_ret = o_ret.reshape(B, S, RET_WIDTH).astype(x.dtype) * ret_norm_w[l]
        o_ret = jax.nn.silu(rg) * o_ret
        mq = rotary(mq.reshape(B, S, MOBA_HEADS, MOBA_HEAD_DIM), ROT_DIM, ROPE_THETA)
        mk = rotary(mk.reshape(B, S, MOBA_HEADS, MOBA_HEAD_DIM), ROT_DIM, ROPE_THETA)
        mv = mv.reshape(B, S, MOBA_HEADS, MOBA_HEAD_DIM)
        o_moba = moba_attention(mq, mk, mv)
        merged = jax.nn.sigmoid(g_ret) * (o_ret @ w_ret_up[l]) + jax.nn.sigmoid(g_moba) * (o_moba @ w_moba_up[l])
        x = x + merged @ w_out[l]
        h2 = rmsnorm_2(x, ffn_norm_w[l])
        up = causal_dwconv(h2 @ w_ffn_up[l], conv_w[l], conv_b[l])
        a, b = jnp.split(up, 2, axis=-1)
        x = x + (jax.nn.silu(a) * b) @ w_ffn_down[l]
    return rmsnorm_2(x, final_norm_w)


def setup_inputs(seed=0):
    out = dict(first_inputs(seed))
    for name, value in second_inputs(seed + 1).items():
        if name != "x":
            out[name + "_2"] = value
    return out


def reference(
    x, norm_attn, w_in, lambda_qk, subln, w_out, norm_ffn, w_gate, w_up, w_down, norm_final,
    attn_norm_w_2, w_in_2, ret_norm_w_2, w_ret_up_2, w_moba_up_2, w_out_2, ffn_norm_w_2,
    w_ffn_up_2, conv_w_2, conv_b_2, w_ffn_down_2, final_norm_w_2,
):
    x = first_block(
        x, norm_attn, w_in, lambda_qk, subln, w_out, norm_ffn, w_gate, w_up, w_down, norm_final,
    )
    return second_block(
        x, attn_norm_w_2, w_in_2, ret_norm_w_2, w_ret_up_2, w_moba_up_2, w_out_2, ffn_norm_w_2,
        w_ffn_up_2, conv_w_2, conv_b_2, w_ffn_down_2, final_norm_w_2,
    )


_drawn_inputs = setup_inputs


def setup_inputs(seed=0):
    import zlib

    import numpy as np

    out = dict(_drawn_inputs(seed))
    spreads = {}
    factors = {'lambda_qk': 8.0,
     'subln': 3.861,
     'norm_ffn': 3.301,
     'ret_norm_w_2': 3.313,
     'conv_b_2': 8.0}
    for name, (base, spread) in spreads.items():
        noise = np.random.default_rng([zlib.crc32(name.encode()), seed]).standard_normal(out[name].shape)
        drawn = base * np.exp(spread * noise) if base else spread * noise
        out[name] = __import__('jax').numpy.asarray(drawn.astype(out[name].dtype))
    for name, factor in factors.items():
        out[name] = (out[name] * factor).astype(out[name].dtype)
    return out
```

```python
from contextlib import ExitStack

import numpy as np

import concourse.bass as bass
from concourse import mybir
from concourse.alu_op_type import AluOpType as ALU

F32 = mybir.dt.float32
F32R = mybir.dt.float32r
ACT = mybir.ActivationFunctionType
AX_X = mybir.AxisListType.X

P = 128
S = 256
TOK = S // P
D = 2048
KD = D // P
N = 512
C = 4
Q = D // N
FF = 5632
NF = FF // N
HD = 128
RD = 256
RING = 4
LEAD = RING - 1
NEG = -1e30
LAM_INIT = 0.8 - 0.6 * 1.0

KIND = "AABBRRMM"
HEADS = [2 if k == "R" else 4 for k in KIND]
HEAD0 = [sum(HEADS[:r]) for r in range(len(KIND))]

ROUND_T = [0, 12, 28, 40, 196, 212, 228, 240]
DOWN_T = [24, 52, 56, 60]
FFN1_T = 64
MERGE_T = 252
FFN2_T = 316
TILES = 448
WINDOW = [12, 24, 40, 52, 208, 224, 240, 252]
ROUND_G = [0, 3, 10, 13, 94, 98, 102, 105]
DOWN_G = [6, 16, 20, 24]
FFN1_G = 28
MERGE_G = 108
FFN2_G = 140
LAST_G = FFN2_G + 6 * NF - 4
assert FFN1_T + 4 * 3 * NF == ROUND_T[4] and FFN2_T + 4 * 3 * NF == TILES

Y_SLOTS = 3

G_ATTN1, G_FFN1, G_ATTN2, G_FFN2, G_FINAL, G_RET, G_SUBLN = 0, 16, 32, 48, 64, 80, 88
N_GAINS = 89


def plan_misc_banks():
    used = [0] * 4
    before = {}

    def piece(key, banks):
        before[key] = {b: used[b] for b in banks}
        for b in banks:
            used[b] += 1

    def xt(phase, q):
        piece(("xt", phase, q), (0, 1) if q % 2 == 0 else (2, 3))

    def attention(r, s):
        if KIND[r] == "R":
            if 0 <= s < 2:
                piece(("scores", r, s), (s,))
            if 1 <= s < 3:
                piece(("values", r, s - 1), (s + 1,))
            if s == 5:
                piece(("out", r), (2, 3))
            return
        if 2 <= s < 6:
            piece(("probs", r, s - 2), (2,))
        if 0 <= s < 4:
            piece(("scores", r, s), (0, 1) if KIND[r] == "B" else (0,))
        if 3 <= s < 7:
            piece(("values", r, s - 3), (3,))
        if KIND[r] == "B" and s == 7:
            piece(("out", r), (2, 3))

    def steps(t0, t1):
        for t in range(t0, t1):
            for r in range(8):
                attention(r, t - WINDOW[r])
                if t in (ROUND_T[r] + 4, ROUND_T[r] + 8):
                    piece(("turn", r, (t - ROUND_T[r]) // 4 - 1), (0, 1))
            for phase, t_last in ((1, DOWN_T[3]), (3, MERGE_T + 60)):
                if 1 <= t - t_last < 5:
                    xt(phase, t - t_last - 1)

    for q in range(Q):
        xt(0, q)
    steps(0, FFN1_T + 1)
    for i in range(NF):
        piece(("ffn1", i), (0, 1))
        if i == 0:
            first = dict(before[("ffn1", 0)])
    assert before[("ffn1", NF - 1)] == {b: first[b] + NF - 1 for b in first}
    for q in range(3):
        xt(2, q)
    xt(2, 3)
    steps(ROUND_T[4], MERGE_T + 12)
    for n in range(Q):
        piece(("merge", n), (0, 1))
    steps(MERGE_T + 12, FFN2_T + 1)
    for i in range(NF):
        piece(("ffn2a", i), (0, 1))
        piece(("ffn2b", i), (2, 3))
    return before


def build(nc, ins, out):
    ctx = ExitStack()
    base = 16512

    def place(name, shape, dtype, at):
        return nc.alloc_sbuf_tensor_at(name, shape, dtype, offset=at)

    KB = 1024
    raw = place("w_raw", [P, RING, C, N], F32, base)
    w_hi = place("w_hi", [P, RING, C, N], F32R, base + 32 * KB)
    w_lo = place("w_lo", [P, RING, C, N], F32R, base + 64 * KB)
    x = place("x", [P, TOK, D], F32, base + 96 * KB)
    xt_hi = place("xt_hi", [P, KD, S], F32R, base + 112 * KB)
    xt_lo = place("xt_lo", [P, KD, S], F32R, base + 128 * KB)
    ph = base + 144 * KB
    yt_hi = place("yt_hi", [P, Y_SLOTS, C, S], F32R, ph)
    yt_lo = place("yt_lo", [P, Y_SLOTS, C, S], F32R, ph + 12 * KB)
    shift = 8 * KB
    stage1 = place("qk_stage1", [P, TOK, N], F32, ph + 16 * KB + shift)
    qt1 = place("q_t1", [P, C, S], F32, ph + 20 * KB + shift)
    kt1 = place("k_t1", [P, C, S], F32, ph + 24 * KB + shift)
    v1 = place("v1", [P, TOK, N], F32, ph + 28 * KB + shift)
    probs1 = place("probs1", [P, 2, 2, TOK, S], F32, ph + 40 * KB)
    pt1 = place("probs_t1", [P, TOK, S], F32, ph + 48 * KB)
    ybuf = place("y", [P, TOK, N], F32, ph + 50 * KB)
    mask_a = place("mask_a", [P, TOK, S], F32, ph + 54 * KB)
    mult_a = place("mult_a", [P, TOK, S], F32, ph + 56 * KB)
    junk = place("junk", [P, N], F32, ph + 58 * KB)
    ht_hi = place("ht_hi", [P, C, S], F32R, ph)
    ht_lo = place("ht_lo", [P, C, S], F32R, ph + 4 * KB)
    gate = place("gate", [P, TOK, N], F32, ph + 8 * KB)
    hid = place("hid", [P, TOK, N], F32, ph + 12 * KB)
    ot_hi = place("ot_hi", [P, 8, S], F32R, ph)
    ot_lo = place("ot_lo", [P, 8, S], F32R, ph + 8 * KB)
    stage2 = place("qk_stage2", [P, TOK, N], F32, ph + 16 * KB)
    qt2 = place("q_t2", [P, C, S], F32, ph + 20 * KB)
    kt2 = place("k_t2", [P, C, S], F32, ph + 24 * KB)
    v2 = place("v2", [P, TOK, N], F32, ph + 28 * KB)
    z = ph + 32 * KB
    ret_g = place("ret_gate", [P, TOK, N], F32, z)
    ret_o = place("ret_o", [P, TOK, N], F32, z + 4 * KB)
    final_row = place("final_row", [P, D], F32, z)
    ret_s = place("ret_scores", [P, 2, 384], F32, z + 8 * KB)
    decay = place("decay", [P, 4, 384], F32, z + 11 * KB)
    rope_r = place("rope_r", [P, 2, TOK, RD], F32, z + 17 * KB)
    causal = place("causal", [P, TOK, S], F32, z + 21 * KB)
    mt_o_hi = place("moba_t_hi", [P, 8, S], F32R, z)
    mt_o_lo = place("moba_t_lo", [P, 8, S], F32R, z + 8 * KB)
    probs2 = place("probs2", [P, 2, TOK, S], F32, z + 16 * KB)
    pt2 = place("probs_t2", [P, TOK, S], F32, z + 23 * KB)
    sig_ret = place("sig_ret", [P, TOK, N], F32, ph + 16 * KB)
    sig_moba = place("sig_moba", [P, TOK, N], F32, ph + 20 * KB)
    mg_hi = place("merged_t_hi", [P, C, S], F32R, ph + 24 * KB)
    mg_lo = place("merged_t_lo", [P, C, S], F32R, ph + 28 * KB)
    h2_hi = place("h2_hi", [P, C, S], F32R, ph)
    h2_lo = place("h2_lo", [P, C, S], F32R, ph + 4 * KB)
    ubuf = place("u", [P, TOK, N], F32, ph + 8 * KB)
    conv_a = place("conv_a", [P, C, S], F32, ph + 12 * KB)
    conv_b = place("conv_b", [P, C, S], F32, ph + 16 * KB)
    at = ph + 60 * KB

    def small(name, *shape):
        nonlocal at
        t = place(name, [P, *shape], F32, at)
        at += 4 * int(np.prod(shape))
        at += -at % 32
        return t

    ident = small("ident", P)
    gains = small("gains", N_GAINS)
    taps = small("taps", 4, 2 * FF // P)
    rope_a = small("rope_a", 2, TOK, 32)
    rope_b = small("rope_b", 2, TOK, 16)
    sumsq = small("sumsq", 6, TOK, Q)
    var = small("var", 6, TOK)
    sd = small("sd", 6, TOK)
    rstd = small("rstd", 6, TOK)
    gain2 = small("gain2", KD)
    peak = small("peak", 2, 4)
    npeak = small("npeak", 2, 4)
    den = small("den", 2, 4)
    rden = small("rden", 2, 4)
    hsum = small("head_sumsq", 8)
    hvar = small("head_var", 8)
    hsd = small("head_sd", 8)
    hrs = small("head_rstd", 8)
    lams = small("lams", 4)
    nlam = small("minus_lam", 1)
    sub8 = small("subln_scaled", 1)
    assert at <= 229344
    lq = ybuf[:, 0, 0:256].rearrange("p (a b) -> p a b", a=4)

    acc = ctx.enter_context(nc.psum_tensor("acc", [P, 2, TOK, N], F32))
    misc = ctx.enter_context(nc.psum_tensor("misc", [P, 4, N], F32))

    def sem(name):
        return ctx.enter_context(nc.semaphore(name))

    raw_ready = [sem(f"raw_ready{i}") for i in range(RING)]
    hi_ready = sem("hi_ready")
    lo_ready = sem("lo_ready")
    tile_used = sem("tile_used")
    pair_read = [sem("pair0_read"), sem("pair1_read")]
    drained = [sem(f"misc{b}_drained") for b in range(4)]
    x_loaded = [sem(f"x_loaded{q}") for q in range(Q)]
    ident_loaded = sem("ident_loaded")
    gains_loaded = sem("gains_loaded")
    tables_loaded = sem("tables_loaded")
    lam_loaded = sem("lam_loaded")
    tables2_loaded = sem("tables2_loaded")
    row_loaded = sem("final_row_loaded")
    stored = sem("stored")
    x1_ready = sem("x1_ready")
    out_ready = sem("out_ready")
    xt_turned = sem("xt_turned")
    xt_hi_done = sem("xt_hi_done")
    sumsq_done = sem("sumsq_done")
    var_ready = sem("var_ready")
    sd_ready = sem("sd_ready")
    rstd_ready = sem("rstd_ready")
    stage_roped = sem("stage_roped")
    stage_turned = sem("stage_turned")
    scores_done = sem("scores_done")
    npeak_ready = sem("npeak_ready")
    exp_done = sem("exp_done")
    rden_ready = sem("rden_ready")
    probs_ready = sem("probs_ready")
    probs_turned = sem("probs_turned")
    values_done = sem("values_done")
    yhi_done = sem("y_hi_done")
    ysq_done = sem("y_squares_done")
    hvar_ready = sem("head_var_ready")
    hsd_ready = sem("head_sd_ready")
    y_normed = sem("y_normed")
    y_turned = sem("y_turned")
    out_hi_done = sem("out_hi_done")
    hid_turned = sem("hid_turned")
    hid_hi_done = sem("hid_hi_done")
    merged_ready = sem("merged_ready")
    merged_turned = sem("merged_turned")
    merged_hi_done = sem("merged_hi_done")
    u_turned = sem("u_turned")
    tap2_done = sem("tap2_done")
    tap1_done = sem("tap1_done")
    silu_done = sem("silu_done")
    prod_done = sem("prod_done")
    h2_hi_done = sem("h2_hi_done")
    h2_ready = sem("h2_ready")
    dve_link = sem("dve_link")
    lam_sums_ready = sem("lam_sums_ready")
    lam_exp_done = sem("lam_exp_done")

    before = plan_misc_banks()

    def slot_count(t, k):
        return (t - k % RING) * (16 // RING) + 16

    def group_read(eng, g):
        eng.wait_ge(pair_read[g % 2], g // 2 + 1)

    def x_quarter(eng, stage, q):
        group_read(eng, {1: DOWN_G[3], 2: ROUND_G[4] - 4, 4: FFN2_G - 4, 5: LAST_G}[stage] + q)

    def tile_of(w, row, col):
        return w[bass.ds(row, C * P), bass.ds(col, N)].rearrange("(c p) n -> p c n", p=P)

    QKV_COL = {"A": (0, 1024, 2048), "B": (3072, 4096, 5120),
               "R": (0, 1024, 2048, 3072), "M": (4096, 5120, 6144)}
    GR_COL, GM_COL = 7168, 9216

    def part(r):
        return r % 2

    block = ctx.enter_context(nc.Block())

    @block.sync
    def _(sp):
        xr = ins["x"].rearrange("b (a p) d -> p (b a) d", p=P)
        sp.dma_start(ident[:, :], ins["ident"]).then_inc(ident_loaded, 16)
        for q in range(Q):
            sp.dma_start(x[:, :, q * N:(q + 1) * N], xr[:, :, q * N:(q + 1) * N]).then_inc(x_loaded[q], 16)
            if q == 0:
                sp.dma_start(gains[:, :], ins["gains"]).then_inc(gains_loaded, 16)

        def load(t, k, src):
            if not (isinstance(t, int) and t < RING):
                sp.wait_ge(lo_ready, t - RING + 1)
            sp.dma_start(raw[:, k % RING], src).then_inc(raw_ready[k % RING], 16)

        def project(t0, w, cols, k0=0):
            for g, col in enumerate(cols):
                for j in range(Q):
                    load(t0 + 4 * g + j, j, tile_of(w, j * C * P, col))

        def down(t0, w, row):
            for n in range(Q):
                load(t0 + n, n, tile_of(w, row, n * N))

        w_in, w_out = ins["w_in"][0], ins["w_out"][0]
        for r in range(4):
            project(ROUND_T[r], w_in, [c + part(r) * N for c in QKV_COL[KIND[r]]])
            if r == 1:
                down(DOWN_T[0], w_out, 0)
        for i in range(1, 4):
            down(DOWN_T[i], w_out, i * N)

        w_gate, w_up, w_down = ins["w_gate"][0], ins["w_up"][0], ins["w_down"][0]
        project(FFN1_T, w_gate, [0])
        project(FFN1_T + 4, w_up, [0])
        with sp.Fori(1, NF) as i:
            t = i * 12 + (FFN1_T - 4)
            project(t, w_gate, [i * N])
            project(t + 4, w_up, [i * N])
            down(t + 8, w_down, i * N - N)
        down(ROUND_T[4] - 4, w_down, (NF - 1) * N)

        w_in2 = ins["w_in_2"][0]
        for r in range(4, 8):
            project(ROUND_T[r], w_in2, [c + part(r) * N for c in QKV_COL[KIND[r]]])

        def merge_loads(t, n):
            project(t, w_in2, [n * N + GR_COL])
            project(t + 4, w_in2, [n * N + GM_COL])
            for j in range(2):
                load(t + 8 + j, j, tile_of(ins["w_ret_up_2"][0], j * C * P, n * N))
            for j in range(2):
                load(t + 10 + j, 2 + j, tile_of(ins["w_moba_up_2"][0], j * C * P, n * N))

        merge_loads(MERGE_T, 0)
        for n in range(1, Q):
            t = n * 16 + (MERGE_T - 4)
            merge_loads(t, n)
            down(t + 12, ins["w_out_2"][0], n * N - N)
        down(FFN2_T - 4, ins["w_out_2"][0], (Q - 1) * N)

        w_up2, w_down2 = ins["w_ffn_up_2"][0], ins["w_ffn_down_2"][0]
        project(FFN2_T, w_up2, [0])
        project(FFN2_T + 4, w_up2, [FF])
        with sp.Fori(1, NF) as i:
            t = i * 12 + (FFN2_T - 4)
            project(t, w_up2, [i * N])
            project(t + 4, w_up2, [i * N + FF])
            down(t + 8, w_down2, i * N - N)
        down(TILES - 4, w_down2, (NF - 1) * N)

        orr = out.rearrange("b (a p) d -> a p (b d)", p=P)
        for tok in range(TOK):
            sp.wait_ge(out_ready, tok + 1)
            sp.dma_start(orr[tok], x[:, tok, :]).then_inc(stored, 16)
        sp.wait_ge(stored, 16 * TOK)

    @block.gpsimd
    def _(pool):
        def load(dst, src, signal):
            pool.dma_start(dst, src).then_inc(signal, 16)

        load(rope_a[:], ins["rope_a"], tables_loaded)
        load(rope_b[:], ins["rope_b"], tables_loaded)
        load(mask_a[:], ins["mask_a"], tables_loaded)
        load(mult_a[:], ins["mult_a"], tables_loaded)
        load(taps[:], ins["taps"], tables_loaded)
        load(lq, ins["lambda_qk"].partition_broadcast(P)[:, 0], lam_loaded)
        pool.wait_ge(tile_used, FFN1_T + 1)
        load(final_row[:], ins["norm_final"].partition_broadcast(P), row_loaded)
        load(decay[:], ins["decay"], tables2_loaded)
        load(rope_r[:], ins["rope_r"], tables2_loaded)
        load(causal[:], ins["causal"], tables2_loaded)
        pool.wait_ge(tile_used, FFN2_T + 1)
        load(final_row[:], ins["final_norm_w_2"].partition_broadcast(P), row_loaded)

    @block.tensor
    def _(pe):
        def products(t, k, pair, a_hi, a_lo, first=True, last=True):
            pe.wait_ge(lo_ready, t + 1)
            for tok in range(TOK):
                for j in range(C):
                    hi = a_hi[:, j, tok * P:(tok + 1) * P]
                    lo = a_lo[:, j, tok * P:(tok + 1) * P]
                    bank = acc[:, pair, tok, :]
                    nc.tensor.matmul(bank, hi, w_hi[:, k % RING, j, :], start=first and j == 0, stop=False)
                    nc.tensor.matmul(bank, hi, w_lo[:, k % RING, j, :], start=False, stop=False)
                    end = nc.tensor.matmul(bank, lo, w_hi[:, k % RING, j, :], start=False,
                                           stop=last and j == C - 1)
            end.then_inc(tile_used, 1)

        def pair_free(pair, use):
            if isinstance(use, int) and use == 0:
                return
            pe.wait_ge(pair_read[pair], use)

        def bank_free(b, use):
            if isinstance(use, int) and use == 0:
                return
            pe.wait_ge(drained[b], use)

        def banks_free(key):
            for b, use in before[key].items():
                bank_free(b, use)

        def turn(src, banks):
            for j in range(C):
                for tok in range(TOK):
                    end = nc.tensor.transpose(
                        misc[:, banks[j // 2], (j % 2) * S + tok * P:(j % 2) * S + (tok + 1) * P],
                        src[:, tok, j * P:(j + 1) * P], ident[:, :])
            return end

        def xt_piece(phase, q):
            if phase == 0:
                pe.wait_ge(x_loaded[q], 16)
            else:
                x_quarter(pe, {1: 1, 2: 2, 3: 4}[phase], q)
            banks_free(("xt", phase, q))
            banks = (0, 1) if q % 2 == 0 else (2, 3)
            turn(x[:, :, q * N:(q + 1) * N], banks).then_inc(xt_turned, 1)

        def xt_ready(phase, q):
            for b, use in before[("xt", phase, q)].items():
                pe.wait_ge(drained[b], use + 1)

        def attention(t):
            for r in range(8):
                s = t - WINDOW[r]
                q_t, k_t, v, probs, p_t = (qt1, kt1, v1, probs1, pt1) if r < 4 else (qt2, kt2, v2, probs2, pt2)
                if KIND[r] == "R":
                    if 0 <= s < 2:
                        h = s
                        if h == 0:
                            for j in range(2):
                                for b in (0, 1):
                                    pe.wait_ge(drained[b], before[("turn", r, j)][b] + 1)
                        banks_free(("scores", r, h))
                        for kt in range(TOK):
                            for dc in range(2):
                                end = nc.tensor.matmul(
                                    misc[:, h, kt * S:(kt + 1) * S - kt * P],
                                    k_t[:, 2 * h + dc, kt * P:(kt + 1) * P], q_t[:, 2 * h + dc, kt * P:],
                                    start=dc == 0, stop=dc == 1)
                        end.then_inc(scores_done, 1)
                    if 1 <= s < 3:
                        h = s - 1
                        if h == 0:
                            group_read(pe, ROUND_G[r] + 2)
                        pe.wait_ge(drained[h], before[("scores", r, h)][h] + 1)
                        banks_free(("values", r, h))
                        vh = v[:, :, h * RD:(h + 1) * RD]
                        nc.tensor.matmul(misc[:, 2 + h, 0:RD], ret_s[:, h, 0:P], vh[:, 0, :], start=True, stop=True)
                        nc.tensor.matmul(misc[:, 2 + h, RD:], ret_s[:, h, P:S], vh[:, 0, :], start=True, stop=False)
                        nc.tensor.matmul(misc[:, 2 + h, RD:], ret_s[:, h, S:], vh[:, 1, :], start=False,
                                         stop=True).then_inc(values_done, 1)
                    if s == 5:
                        pe.wait_ge(y_normed, r - 1)
                        banks_free(("out", r))
                        turn(ret_o, (2, 3)).then_inc(y_turned, 1)
                    continue
                if 2 <= s < 6:
                    h = s - 2
                    pe.wait_ge(probs_ready, HEAD0[r] + h + 1 - (4 if r > 5 else 0))
                    banks_free(("probs", r, h))
                    src = probs[:, h % 2, 0] if r < 4 else probs[:, h % 2]
                    for kt in range(TOK):
                        for qt in range(TOK):
                            end = nc.tensor.transpose(misc[:, 2, kt * S + qt * P:kt * S + (qt + 1) * P],
                                                      src[:, qt, kt * P:(kt + 1) * P], ident[:, :])
                    end.then_inc(probs_turned, 1)
                if 0 <= s < 4:
                    h = s
                    if h == 0:
                        for j in range(2):
                            for b in (0, 1):
                                pe.wait_ge(drained[b], before[("turn", r, j)][b] + 1)
                    banks_free(("scores", r, h))
                    if KIND[r] == "B":
                        for c in range(2):
                            rows = slice(c * 64, (c + 1) * 64)
                            for qt in range(TOK):
                                end = nc.tensor.matmul(misc[:, c, qt * S:(qt + 1) * S],
                                                       q_t[rows, h, qt * P:(qt + 1) * P], k_t[rows, h, :],
                                                       start=True, stop=True)
                    else:
                        for qt in range(TOK):
                            end = nc.tensor.matmul(misc[:, 0, qt * S:(qt + 1) * S],
                                                   q_t[:, h, qt * P:(qt + 1) * P], k_t[:, h, :],
                                                   start=True, stop=True)
                    end.then_inc(scores_done, 1)
                if 3 <= s < 7:
                    h = s - 3
                    if h == 0:
                        group_read(pe, ROUND_G[r] + 2)
                    pe.wait_ge(drained[2], before[("probs", r, h)][2] + 1)
                    banks_free(("values", r, h))
                    if KIND[r] != "B":
                        for kt in range(TOK):
                            end = nc.tensor.matmul(misc[:, 3, 0:S], v[:, kt, h * HD:(h + 1) * HD], p_t[:, kt, :],
                                                   start=kt == 0, stop=kt == 1)
                    else:
                        for qt in range(TOK):
                            for kt in range(TOK):
                                end = nc.tensor.matmul(misc[:, 3, qt * HD:(qt + 1) * HD],
                                                       p_t[:, kt, qt * P:(qt + 1) * P],
                                                       v[:, kt, h * HD:(h + 1) * HD],
                                                       start=kt == 0, stop=kt == 1)
                    end.then_inc(values_done, 1)
                if KIND[r] == "B" and s == 7:
                    pe.wait_ge(y_normed, r - 1)
                    banks_free(("out", r))
                    turn(ybuf, (2, 3)).then_inc(y_turned, 1)

        def stage_turn(t):
            for r in range(8):
                j = (t - ROUND_T[r]) // 4 - 1
                if t in (ROUND_T[r] + 4, ROUND_T[r] + 8):
                    n = 2 * r + j
                    pe.wait_ge(stage_roped, n + 1)
                    banks_free(("turn", r, j))
                    turn(stage1 if r < 4 else stage2, (0, 1)).then_inc(stage_turned, 1)

        def small_pieces(t):
            attention(t)
            stage_turn(t)
            for phase, t_last in ((1, DOWN_T[3]), (3, FFN2_T - 4)):
                if 1 <= t - t_last < 5:
                    xt_piece(phase, t - t_last - 1)

        def project(t0, pair, use, phase=None, a=(xt_hi, xt_lo), tiles=Q, after=None, wait=None, k0=0):
            pair_free(pair, use)
            if wait:
                wait()
            for j in range(tiles):
                if phase is not None:
                    xt_ready(phase, j)
                products(t0 + j, k0 + j, pair, a[0][:, C * j:C * (j + 1)], a[1][:, C * j:C * (j + 1)],
                         first=j == 0, last=j == tiles - 1)
                if after:
                    after(t0 + j)

        def down(t0, pair0, use0, a_hi, a_lo, after=None):
            for n in range(Q):
                pair = (pair0 + n) % 2
                pair_free(pair, use0 + (pair0 + n) // 2)
                products(t0 + n, n, pair, a_hi, a_lo)
                if after:
                    after(t0 + n)

        def at_first(piece):
            seen = []

            def after(t):
                if not seen:
                    piece()
                seen.append(t)
            return after

        pe.wait_ge(ident_loaded, 16)
        for q in range(Q):
            xt_piece(0, q)

        def block_round(r, phase, groups):
            for g in range(groups):
                n = ROUND_G[r] + g
                project(ROUND_T[r] + 4 * g, n % 2, n // 2, phase if g == 0 else None, after=small_pieces)

        def y_ready(i):
            if KIND[i] == "B":
                for b in (2, 3):
                    pe.wait_ge(drained[b], before[("out", i)][b] + 1)
            else:
                pe.wait_ge(drained[3], before[("values", i, 3)][3] + 1)

        def block_down(i):
            y_ready(i)
            s = i % Y_SLOTS
            down(DOWN_T[i], DOWN_G[i] % 2, DOWN_G[i] // 2, yt_hi[:, s], yt_lo[:, s], after=small_pieces)

        for r in range(4):
            block_round(r, 0 if r == 0 else None, 3)
            if r == 1:
                block_down(0)
        for i in range(1, 4):
            block_down(i)

        def hid_turn(i, use):
            pe.wait_ge(pair_read[1], use + 1)
            for b in (0, 1):
                bank_free(b, before[("ffn1", 0)][b] + i)
            turn(hid, (0, 1)).then_inc(hid_turned, 1)

        def ffn1_down(t, use, i, after=None):
            for b in (0, 1):
                pe.wait_ge(drained[b], before[("ffn1", 0)][b] + i + 1)
            down(t, 0, use, ht_hi, ht_lo, after)

        g = FFN1_G // 2
        project(FFN1_T, 0, g, 1, after=small_pieces)
        project(FFN1_T + 4, 1, g)
        hid_turn(0, g)
        with pe.Fori(1, NF) as i:
            t = i * 12 + (FFN1_T - 4)
            use = i * 3 + (g - 2)
            project(t, 0, use)
            project(t + 4, 1, use)
            ffn1_down(t + 8, use + 1, i - 1, after=at_first(lambda: hid_turn(i, use)))
        ffn1_down(ROUND_T[4] - 4, g - 2 + 3 * NF, NF - 1,
                  after=lambda t: xt_piece(2, t - ROUND_T[4] + 3) if t > ROUND_T[4] - 4 else None)

        for r in range(4, 8):
            for gi in range(HEADS[r] == 2 and 4 or 3):
                n = ROUND_G[r] + gi

                def after(t):
                    if t == ROUND_T[4]:
                        xt_piece(2, 3)
                    small_pieces(t)

                project(ROUND_T[r] + 4 * gi, n % 2, n // 2, 2 if (r == 4 and gi == 0) else None, after=after)

        def ret_ready():
            for r in (4, 5):
                for b in (2, 3):
                    pe.wait_ge(drained[b], before[("out", r)][b] + 1)

        def moba_ready():
            pe.wait_ge(drained[3], before[("values", 7, 3)][3] + 1)

        def merge(t, use, peeled):
            after = small_pieces if peeled else None
            project(t, 0, use, after=after)
            project(t + 4, 1, use, after=after)
            project(t + 8, 0, use + 1, a=(ot_hi, ot_lo), tiles=2, after=after, wait=ret_ready if peeled else None)
            project(t + 10, 1, use + 1, a=(mt_o_hi, mt_o_lo), tiles=2, after=after,
                    wait=moba_ready if peeled else None, k0=2)

        def merged_turn(n):
            pe.wait_ge(merged_ready, n + 1)
            for b in (0, 1):
                bank_free(b, before[("merge", 0)][b] + n)
            turn(sig_moba, (0, 1)).then_inc(merged_turned, 1)

        def merge_down(t, use, n, after=None):
            for b in (0, 1):
                pe.wait_ge(drained[b], before[("merge", 0)][b] + n + 1)
            down(t, 0, use, mg_hi, mg_lo, after)

        g = MERGE_G // 2
        merge(MERGE_T, g, True)
        merged_turn(0)
        with pe.Fori(1, Q) as n:
            t = n * 16 + (MERGE_T - 4)
            use = n * 4 + (g - 2)
            merge(t, use, False)
            merge_down(t + 12, use + 2, n - 1, after=at_first(lambda: merged_turn(n)))
        merge_down(FFN2_T - 4, g - 2 + 4 * Q, Q - 1, after=small_pieces)

        def u_turn(i, half, use):
            pe.wait_ge(pair_read[half], use + 1)
            key = ("ffn2a", 0) if half == 0 else ("ffn2b", 0)
            for b in before[key]:
                bank_free(b, before[key][b] + i)
            turn(ubuf, (2 * half, 2 * half + 1)).then_inc(u_turned, 1)

        def ffn2_down(t, use, i, after=None):
            pe.wait_ge(h2_ready, i + 1)
            down(t, 0, use, h2_hi, h2_lo, after)

        g = FFN2_G // 2
        project(FFN2_T, 0, g, 3, after=small_pieces)
        project(FFN2_T + 4, 1, g, after=at_first(lambda: u_turn(0, 0, g)))
        u_turn(0, 1, g)
        with pe.Fori(1, NF) as i:
            t = i * 12 + (FFN2_T - 4)
            use = i * 3 + (g - 2)
            project(t, 0, use)
            project(t + 4, 1, use, after=at_first(lambda: u_turn(i, 0, use)))
            ffn2_down(t + 8, use + 1, i - 1, after=at_first(lambda: u_turn(i, 1, use)))
        ffn2_down(TILES - 4, g - 2 + 3 * NF, NF - 1)

    @block.scalar
    def _(act):
        def split(t, k):
            if isinstance(t, int) and t >= TILES:
                return
            act.wait_ge(raw_ready[k % RING], slot_count(t, k))
            if not (isinstance(t, int) and t < RING):
                act.wait_ge(tile_used, t - RING + 1)
            nc.scalar.activation(w_hi[:, k % RING], raw[:, k % RING], ACT.Copy).then_inc(hi_ready, 1)

        def copy(dst, src, scale=1.0, func=ACT.Copy, **kw):
            return nc.scalar.activation(dst, src, func, scale=scale, **kw)

        def read_group(t, pair, dst, scales, func=ACT.Copy):
            act.wait_ge(tile_used, t + 1)
            copy(dst[:, 0, :], acc[:, pair, 0, :], scales[:, 0:1], func)
            copy(dst[:, 1, :], acc[:, pair, 1, :], scales[:, 1:2], func).then_inc(pair_read[pair], 1)

        def xt_hi_piece(phase, q):
            act.wait_ge(xt_turned, 4 * phase + q + 1)
            gain = {0: gains[:, G_ATTN1:], 1: gains[:, G_FFN1:], 2: gain2[:, :], 3: gains[:, G_FFN2:]}[phase]
            banks = (0, 1) if q % 2 == 0 else (2, 3)
            for j in range(C):
                end = copy(xt_hi[:, C * q + j, :], misc[:, banks[j // 2], (j % 2) * S:(j % 2 + 1) * S],
                           gain[:, C * q + j:C * q + j + 1])
                if j % 2:
                    end.then_inc(xt_hi_done, 1)

        squares = [0]

        def square_sum(zn, tok, q):
            if squares[0]:
                act.wait_ge(sumsq_done, squares[0])
            nc.scalar.activation(junk[:, :], x[:, tok, q * N:(q + 1) * N], ACT.Square,
                                 accum_out=sumsq[:, zn, tok, q:q + 1]).then_inc(sumsq_done, 1)
            squares[0] += 1

        def root(zn):
            act.wait_ge(var_ready, zn + 1)
            nc.scalar.activation(sd[:, zn, :], var[:, zn, :], ACT.Sqrt).then_inc(sd_ready, 1)

        def attention(t):
            for r in range(8):
                s = t - WINDOW[r]
                probs, p_t, v = (probs1, pt1, v1) if r < 4 else (probs2, pt2, v2)
                head = HEAD0[r] - (4 if r > 5 else 0)
                head_am = head - (8 if r > 5 else 0)
                if KIND[r] == "R":
                    if 1 <= s < 3:
                        h = s - 1
                        act.wait_ge(values_done, HEAD0[r] + h + 1)
                        for qt in range(TOK):
                            src = misc[:, 2 + h, qt * RD:(qt + 1) * RD]
                            if ysquares[0] > 0:
                                act.wait_ge(ysq_done, ysquares[0])
                            nc.scalar.activation(junk[:, 0:RD], src, ACT.Square,
                                                 accum_out=hsum[:, 2 * h + qt:2 * h + qt + 1]).then_inc(ysq_done, 1)
                            ysquares[0] += 1
                        copy(ret_o[:, :, h * RD:(h + 1) * RD],
                             misc[:, 2 + h, :].rearrange("p (a b) -> p a b", a=TOK)).then_inc(drained[2 + h], 1)
                    if s == 3:
                        act.wait_ge(tile_used, t + 1)
                        n = ROUND_G[r] + 3
                        read_group(t, n % 2, ret_g, rstd[:, 3, :], ACT.Silu)
                        act.wait_ge(hvar_ready, r - 1)
                        nc.scalar.activation(hsd[:, 0:4], hvar[:, 0:4], ACT.Sqrt).then_inc(hsd_ready, 1)
                    if s == 5:
                        act.wait_ge(y_turned, r - 1)
                        for j in range(C):
                            c = 4 * (r - 4) + j
                            end = copy(ot_hi[:, c, :], misc[:, 2 + j // 2, (j % 2) * S:(j % 2 + 1) * S],
                                       gains[:, G_RET + c:G_RET + c + 1])
                            if j % 2:
                                end.then_inc(out_hi_done, 1)
                    continue
                if KIND[r] != "B" and 1 <= s < 5:
                    h = s - 1
                    act.wait_ge(rden_ready, head_am + h + 1)
                    for qt in range(TOK):
                        p = probs[:, h % 2, 0, qt, :] if r < 4 else probs[:, h % 2, qt, :]
                        end = copy(p, p, rden[:, h % 2, qt:qt + 1])
                    end.then_inc(probs_ready, 1)
                if 2 <= s < 6:
                    h = s - 2
                    act.wait_ge(probs_turned, head + h + 1)
                    if head + h > 0:
                        act.wait_ge(values_done, HEAD0[r] + h)
                    copy(p_t[:, :, :], misc[:, 2, :].rearrange("p (a b) -> p a b", a=TOK)).then_inc(drained[2], 1)
                if 0 <= s < 4:
                    h = s
                    n = head + h
                    act.wait_ge(npeak_ready, n + 1)
                    if KIND[r] == "B":
                        if h >= 2:
                            act.wait_ge(probs_turned, n - 1)
                        for c in range(2):
                            for qt in range(TOK):
                                k = 2 * c + qt
                                end = nc.scalar.activation(
                                    probs[:, h % 2, c, qt, :], misc[:, c, qt * S:(qt + 1) * S], ACT.Exp,
                                    bias=npeak[:, h % 2, k:k + 1], scale=64 ** -0.5,
                                    accum_out=den[:, h % 2, k:k + 1])
                            end.then_inc(drained[c], 1)
                    else:
                        for qt in range(TOK):
                            p = probs[:, h % 2, 0, qt, :] if r < 4 else probs[:, h % 2, qt, :]
                            kw = {"accum_out": den[:, h % 2, qt:qt + 1]} if KIND[r] == "M" else {}
                            end = nc.scalar.activation(p, p, ACT.Exp, bias=npeak[:, h % 2, qt:qt + 1], **kw)
                        end.then_inc(exp_done, 1)
                if 3 <= s < 7:
                    h = s - 3
                    act.wait_ge(values_done, HEAD0[r] + h + 1)
                    if KIND[r] == "B":
                        copy(ybuf[:, :, h * HD:(h + 1) * HD],
                             misc[:, 3, 0:S].rearrange("p (a b) -> p a b", a=TOK)).then_inc(drained[3], 1)
                    else:
                        if r < 4:
                            dst = yt_hi[:, r % Y_SLOTS, h, :]
                        else:
                            dst = mt_o_hi[:, 4 * (r - 6) + h, :]
                        copy(dst, misc[:, 3, 0:S]).then_inc(yhi_done, 1)
                if KIND[r] == "B" and s == 6:
                    act.wait_ge(drained[3], before[("values", r, 3)][3] + 1)
                    act.wait_ge(probs_turned, head + 4)
                    nc.scalar.activation(probs1[:, 0].rearrange("p c a b -> p (c a b)"),
                                         ybuf[:, :, :].rearrange("p a b -> p (a b)"),
                                         ACT.Square).then_inc(ysq_done, 1)
                    ysquares[0] += 1
                    act.wait_ge(hvar_ready, r - 1)
                    nc.scalar.activation(hsd[:, :], hvar[:, :], ACT.Sqrt).then_inc(hsd_ready, 1)
                if KIND[r] == "B" and s == 7:
                    act.wait_ge(y_turned, r - 1)
                    for b in range(2):
                        copy(yt_hi[:, r % Y_SLOTS, 2 * b:2 * b + 2, :],
                             misc[:, 2 + b, :].rearrange("p (a b) -> p a b", a=2), sub8[:, 0:1]).then_inc(out_hi_done, 1)

        ysquares = [0]

        def projections(t):
            for r in range(8):
                rs = rstd[:, 0, :] if r < 4 else rstd[:, 3, :]
                for j in range(2):
                    if t == ROUND_T[r] + 4 * j + 3:
                        n = ROUND_G[r] + j
                        if 2 * r + j > 0:
                            act.wait_ge(stage_turned, 2 * r + j)
                        act.wait_ge(tile_used, t + 1)
                        st = stage1 if r < 4 else stage2
                        copy(st[:, 0, :], acc[:, n % 2, 0, :], rs[:, 0:1])
                        copy(st[:, 1, :], acc[:, n % 2, 1, :], rs[:, 1:2]).then_inc(pair_read[n % 2], 1)
                    if t == ROUND_T[r] + 4 * j + 4:
                        act.wait_ge(stage_turned, 2 * r + j + 1)
                        dst = (qt1, kt1)[j] if r < 4 else (qt2, kt2)[j]
                        copy(dst[:, 0:2, :], misc[:, 0, :].rearrange("p (a b) -> p a b", a=2)).then_inc(drained[0], 1)
                if t == ROUND_T[r] + 11:
                    n = ROUND_G[r] + 2
                    act.wait_ge(tile_used, t + 1)
                    vv = v1 if r < 4 else v2
                    copy(vv[:, 0, :], acc[:, n % 2, 0, :], rs[:, 0:1])
                    copy(vv[:, 1, :], acc[:, n % 2, 1, :], rs[:, 1:2]).then_inc(pair_read[n % 2], 1)

        def pieces(t):
            attention(t)
            projections(t)
            for phase, t_last in ((1, DOWN_T[3]), (3, FFN2_T - 4)):
                if 1 <= t - t_last < 5:
                    xt_hi_piece(phase, t - t_last - 1)
                if 0 <= t - t_last < 4:
                    zn = {1: 1, 3: 4}[phase]
                    x_quarter(act, zn, t - t_last)
                    for tok in range(TOK):
                        square_sum(zn, tok, t - t_last)

        for t in range(LEAD):
            split(t, t)
        act.wait_ge(gains_loaded, 16)
        for q in range(Q):
            xt_hi_piece(0, q)
        for q in range(Q):
            act.wait_ge(x_loaded[q], 16)
            for tok in range(TOK):
                square_sum(0, tok, q)
        root(0)
        act.wait_ge(rstd_ready, 1)
        act.wait_ge(lam_sums_ready, 1)
        nc.scalar.activation(lams[:, 2:4], lams[:, 0:2], ACT.Exp).then_inc(lam_exp_done, 1)

        for t in range(FFN1_T):
            split(t + LEAD, t + LEAD)
            pieces(t)

        def read_gate(t):
            act.wait_ge(tile_used, t + 1)
            copy(gate[:, 0, :], acc[:, 0, 0, :], rstd[:, 1, 0:1], ACT.Silu)
            copy(gate[:, 1, :], acc[:, 0, 1, :], rstd[:, 1, 1:2], ACT.Silu).then_inc(pair_read[0], 1)

        def hid_hi(i):
            act.wait_ge(hid_turned, i + 1)
            for b in range(2):
                copy(ht_hi[:, 2 * b:2 * b + 2, :],
                     misc[:, b, :].rearrange("p (a b) -> p a b", a=2)).then_inc(hid_hi_done, 1)

        for k in range(8):
            split(FFN1_T + k + LEAD, k + LEAD)
            if k == 0:
                pieces(FFN1_T)
            if k == 1:
                root(1)
            if k == 3:
                act.wait_ge(rstd_ready, 2)
                read_gate(FFN1_T + k)
        hid_hi(0)
        with act.Fori(1, NF) as i:
            t = i * 12 + (FFN1_T - 4)
            for k in range(12):
                split(t + k + LEAD, k + LEAD)
                if k == 3:
                    act.wait_ge(pair_read[1], i * 3 + (FFN1_G // 2 - 3))
                    read_gate(t + k)
                if k == 11:
                    act.wait_ge(tile_used, t + k + 1)
                    hid_hi(i)
        for k in range(4):
            t = ROUND_T[4] - 4 + k
            split(t + LEAD, k + LEAD)
            x_quarter(act, 2, k)
            for tok in range(TOK):
                square_sum(2, tok, k)
            if k > 0:
                xt_hi_piece(2, k - 1)

        for t in range(ROUND_T[4], MERGE_T):
            split(t + LEAD, t + LEAD)
            if t == ROUND_T[4]:
                xt_hi_piece(2, 3)
                root(2)
            if t == ROUND_T[4] + 2:
                for q in range(Q):
                    for tok in range(TOK):
                        act.wait_ge(x1_ready, tok + 1)
                        square_sum(3, tok, q)
                root(3)
            if t == ROUND_T[4] + 3:
                act.wait_ge(rstd_ready, 4)
            pieces(t)

        def sigmoid(t, pair, dst):
            act.wait_ge(tile_used, t + 1)
            copy(dst[:, 0, :], acc[:, pair, 0, :], rstd[:, 3, 0:1], ACT.Sigmoid)
            copy(dst[:, 1, :], acc[:, pair, 1, :], rstd[:, 3, 1:2], ACT.Sigmoid).then_inc(pair_read[pair], 1)

        def merged_hi(n):
            act.wait_ge(merged_turned, n + 1)
            for b in range(2):
                copy(mg_hi[:, 2 * b:2 * b + 2, :],
                     misc[:, b, :].rearrange("p (a b) -> p a b", a=2)).then_inc(merged_hi_done, 1)

        for k in range(12):
            t = MERGE_T + k
            split(t + LEAD, k + LEAD)
            if k == 7:
                act.wait_ge(scores_done, HEAD0[7] + 4)
            if k in (3, 7):
                sigmoid(t, k // 4, (sig_ret, sig_moba)[k // 4])
            pieces(t)
        act.wait_ge(values_done, HEAD0[7] + 4)
        merged_hi(0)
        with act.Fori(1, Q) as n:
            t = n * 16 + (MERGE_T - 4)
            for k in range(16):
                split(t + k + LEAD, k + LEAD)
                if k == 3:
                    act.wait_ge(merged_ready, n)
                    sigmoid(t + k, 0, sig_ret)
                if k == 7:
                    act.wait_ge(merged_turned, n)
                    sigmoid(t + k, 1, sig_moba)
                if k == 15:
                    act.wait_ge(tile_used, t + k + 1)
                    merged_hi(n)
        for k in range(4):
            t = FFN2_T - 4 + k
            split(t + LEAD, k + LEAD)
            pieces(t)

        def u_copy(i, half, t):
            act.wait_ge(u_turned, i * 2 + half)
            act.wait_ge(tile_used, t + 1)
            copy(ubuf[:, 0, :], acc[:, half, 0, :], rstd[:, 4, 0:1])
            copy(ubuf[:, 1, :], acc[:, half, 1, :], rstd[:, 4, 1:2]).then_inc(pair_read[half], 1)

        def last_tap(i, half, dst):
            act.wait_ge(u_turned, i * 2 + half + 1)
            for j in range(C):
                col = i * C + (half * FF // P + j)
                src = misc[:, 2 * half + j // 2, (j % 2) * S:(j % 2 + 1) * S]
                end = nc.scalar.activation(dst[:, j, :], src, ACT.Identity, bias=taps[:, 3, bass.ds(col, 1)],
                                           scale=taps[:, 2, bass.ds(col, 1)])
                if j % 2:
                    end.then_inc(tap2_done, 1)

        def silu_a(i):
            act.wait_ge(drained[1], i + (before[("ffn2a", 0)][1] + 1))
            nc.scalar.activation(conv_a[:], conv_a[:], ACT.Silu).then_inc(silu_done, 1)

        def product_hi(i):
            act.wait_ge(prod_done, i + 1)
            copy(h2_hi[:], conv_a[:]).then_inc(h2_hi_done, 1)

        for k in range(8):
            t = FFN2_T + k
            split(t + LEAD, k + LEAD)
            if k == 0:
                pieces(t)
            if k == 1:
                root(4)
            if k == 3:
                act.wait_ge(rstd_ready, 5)
                act.wait_ge(tile_used, t + 1)
                copy(ubuf[:, 0, :], acc[:, 0, 0, :], rstd[:, 4, 0:1])
                copy(ubuf[:, 1, :], acc[:, 0, 1, :], rstd[:, 4, 1:2]).then_inc(pair_read[0], 1)
            if k == 5:
                last_tap(0, 0, conv_a)
            if k == 6:
                silu_a(0)
            if k == 7:
                u_copy(0, 1, t)
                last_tap(0, 1, conv_b)
                product_hi(0)
        with act.Fori(1, NF) as i:
            t = i * 12 + (FFN2_T - 4)
            for k in range(12):
                split(t + k + LEAD, k + LEAD)
                if k == 3:
                    u_copy(i, 0, t + k)
                if k == 5:
                    act.wait_ge(h2_ready, i)
                    last_tap(i, 0, conv_a)
                if k == 6:
                    silu_a(i)
                if k == 7:
                    u_copy(i, 1, t + k)
                if k == 8:
                    last_tap(i, 1, conv_b)
                if k == 11:
                    act.wait_ge(tile_used, t + k + 1)
                    product_hi(i)
        for k in range(4):
            t = TILES - 4 + k
            split(t + LEAD, k + LEAD)
            x_quarter(act, 5, k)
            for tok in range(TOK):
                square_sum(5, tok, k)
        root(5)

    @block.vector
    def _(dve):
        links = [0]

        def link(ins_):
            ins_.then_inc(dve_link, 1)
            links[0] += 1
            dve.wait_ge(dve_link, links[0])

        def split(t, k):
            if isinstance(t, int) and t >= TILES:
                return
            dve.wait_ge(raw_ready[k % RING], slot_count(t, k))
            dve.wait_ge(hi_ready, t + 1)
            nc.vector.tensor_tensor(w_lo[:, k % RING], raw[:, k % RING], w_hi[:, k % RING].bitcast(F32),
                                    ALU.subtract).then_inc(lo_ready, 1)

        def minus_hi(dst, src, hi, gain=None):
            if gain is None:
                return nc.vector.tensor_tensor(dst, src, hi.bitcast(F32), ALU.subtract)
            return nc.vector.scalar_tensor_tensor(out=dst, in0=src, scalar=gain, in1=hi.bitcast(F32),
                                                  op0=ALU.mult, op1=ALU.subtract)

        def xt_lo_piece(phase, q):
            gain = {0: gains[:, G_ATTN1:], 1: gains[:, G_FFN1:], 2: gain2[:, :], 3: gains[:, G_FFN2:]}[phase]
            banks = (0, 1) if q % 2 == 0 else (2, 3)
            for j in range(C):
                if j % 2 == 0:
                    dve.wait_ge(xt_hi_done, 2 * (4 * phase + q) + j // 2 + 1)
                c = C * q + j
                end = minus_hi(xt_lo[:, c, :], misc[:, banks[j // 2], (j % 2) * S:(j % 2 + 1) * S],
                               xt_hi[:, c, :], gain[:, c:c + 1])
                if j % 2:
                    end.then_inc(drained[banks[j // 2]], 1)

        def add_group(t, pair, n):
            dve.wait_ge(tile_used, t + 1)
            for tok in range(TOK):
                xs = x[:, tok, n * N:(n + 1) * N]
                end = nc.vector.tensor_tensor(xs, acc[:, pair, tok, :], xs, ALU.add)
            end.then_inc(pair_read[pair], 1)

        def variance(zn):
            dve.wait_ge(sumsq_done, 8 * (zn + 1))
            link(nc.vector.tensor_reduce(var[:, zn, :], sumsq[:, zn], AX_X, ALU.add))
            nc.vector.tensor_scalar(var[:, zn, :], var[:, zn, :], 1.0 / D, 1e-6, ALU.mult,
                                    ALU.add).then_inc(var_ready, 1)

        def inverse(zn):
            dve.wait_ge(sd_ready, zn + 1)
            if zn != 3:
                nc.vector.reciprocal(rstd[:, zn, :], sd[:, zn, :]).then_inc(rstd_ready, 1)
            else:
                link(nc.vector.reciprocal(rstd[:, zn, :], sd[:, zn, :]))
                nc.vector.tensor_tensor(rstd[:, zn, :], rstd[:, zn, :], rstd[:, 2, :],
                                        ALU.mult).then_inc(rstd_ready, 1)

        def rope(r, j):
            n = 2 * r + j
            g = ROUND_G[r] + j
            st = stage1 if r < 4 else stage2
            dve.wait_ge(pair_read[g % 2], g // 2 + 1)
            nh, tab = {"A": (4, rope_a), "B": (8, rope_b), "R": (2, rope_r), "M": (4, rope_a)}[KIND[r]]
            rot = tab.shape[-1]
            half = rot // 2
            xs = st[:, :, :].rearrange("p a (h d) -> p a h d", h=nh)
            if KIND[r] == "R":
                tmp = ret_o[:, :, :].rearrange("p a (h d) -> p a h d", h=nh)
            else:
                tmp = junk[:, 0:TOK * nh * rot].rearrange("p (a h d) -> p a h d", a=TOK, h=nh)

            def table(k, lo, hi):
                w = hi - lo
                return tab[:, k, :, lo:hi].unsqueeze(2).to_broadcast([P, TOK, nh, w])

            nc.vector.tensor_tensor(tmp[:, :, :, 0:half], xs[:, :, :, half:rot], table(1, 0, half), ALU.mult)
            link(nc.vector.tensor_tensor(tmp[:, :, :, half:rot], xs[:, :, :, 0:half], table(1, half, rot), ALU.mult))
            link(nc.vector.tensor_tensor(xs[:, :, :, 0:rot], xs[:, :, :, 0:rot], table(0, 0, rot), ALU.mult))
            nc.vector.tensor_tensor(xs[:, :, :, 0:rot], xs[:, :, :, 0:rot], tmp[:, :, :, :],
                                    ALU.add).then_inc(stage_roped, 1)

        def attention(t):
            for r in range(8):
                s = t - WINDOW[r]
                probs = probs1 if r < 4 else probs2
                head = HEAD0[r] - (4 if r > 5 else 0)
                if KIND[r] == "R":
                    if 0 <= s < 2:
                        h = s
                        dve.wait_ge(scores_done, HEAD0[r] + h + 1)
                        if r > 4:
                            dve.wait_ge(values_done, HEAD0[r - 1] + h + 1)
                        nc.vector.tensor_tensor(ret_s[:, h, 0:S], misc[:, h, 0:S],
                                                decay[:, 2 * part(r) + h, 0:S], ALU.mult)
                        nc.vector.tensor_tensor(ret_s[:, h, S:], misc[:, h, S:S + P],
                                                decay[:, 2 * part(r) + h, S:], ALU.mult).then_inc(drained[h], 1)
                    if s == 2:
                        dve.wait_ge(ysq_done, 2 + 4 * (r - 3))
                        nc.vector.tensor_scalar(hvar[:, 0:4], hsum[:, 0:4], 1.0 / RD, 1e-6, ALU.mult,
                                                ALU.add).then_inc(hvar_ready, 1)
                    if s == 4:
                        dve.wait_ge(hsd_ready, r - 1)
                        link(nc.vector.reciprocal(hrs[:, 0:4], hsd[:, 0:4]))
                        n = ROUND_G[r] + 3
                        dve.wait_ge(pair_read[n % 2], n // 2 + 1)
                        for h in range(2):
                            for qt in range(TOK):
                                o = ret_o[:, qt, h * RD:(h + 1) * RD]
                                end = nc.vector.scalar_tensor_tensor(
                                    out=o, in0=o, scalar=hrs[:, 2 * h + qt:2 * h + qt + 1],
                                    in1=ret_g[:, qt, h * RD:(h + 1) * RD], op0=ALU.mult, op1=ALU.mult)
                        end.then_inc(y_normed, 1)
                    if s == 5:
                        for j in range(C):
                            c = 4 * (r - 4) + j
                            if j % 2 == 0:
                                dve.wait_ge(out_hi_done, 2 * (r - 2) + j // 2 + 1)
                            end = minus_hi(ot_lo[:, c, :], misc[:, 2 + j // 2, (j % 2) * S:(j % 2 + 1) * S],
                                           ot_hi[:, c, :], gains[:, G_RET + c:G_RET + c + 1])
                            if j % 2:
                                end.then_inc(drained[2 + j // 2], 1)
                    continue
                if 1 <= s < 5:
                    h = s - 1
                    if KIND[r] == "B":
                        dve.wait_ge(drained[1], before[("scores", r, h)][1] + 1)
                    else:
                        dve.wait_ge(exp_done, head - (8 if r > 5 else 0) + h + 1)
                    if KIND[r] == "A":
                        for qt in range(TOK):
                            p = probs[:, h % 2, 0, qt, :]
                            end = nc.vector.tensor_tensor_reduce(p, p, mult_a[:, qt, :], 1.0, 0.0, ALU.mult,
                                                                 ALU.add, den[:, h % 2, qt:qt + 1])
                        link(end)
                        nc.vector.reciprocal(rden[:, h % 2, 0:2], den[:, h % 2, 0:2]).then_inc(rden_ready, 1)
                    elif KIND[r] == "M":
                        nc.vector.reciprocal(rden[:, h % 2, 0:2], den[:, h % 2, 0:2]).then_inc(rden_ready, 1)
                    else:
                        link(nc.vector.reciprocal(rden[:, h % 2, :], den[:, h % 2, :]))
                        link(nc.vector.tensor_scalar(rden[:, h % 2, 2:4], rden[:, h % 2, 2:4], nlam[:, 0:1], None,
                                                     ALU.mult))
                        for qt in range(TOK):
                            p1 = probs[:, h % 2, 1, qt, :]
                            end = nc.vector.tensor_scalar(p1, p1, rden[:, h % 2, 2 + qt:3 + qt], None, ALU.mult)
                        link(end)
                        for qt in range(TOK):
                            p0 = probs[:, h % 2, 0, qt, :]
                            end = nc.vector.scalar_tensor_tensor(
                                out=p0, in0=p0, scalar=rden[:, h % 2, qt:qt + 1], in1=probs[:, h % 2, 1, qt, :],
                                op0=ALU.mult, op1=ALU.add)
                        end.then_inc(probs_ready, 1)
                if 0 <= s < 4:
                    h = s
                    n = head + h
                    dve.wait_ge(scores_done, HEAD0[r] + h + 1)
                    if KIND[r] == "B":
                        for c in range(2):
                            end = nc.vector.tensor_reduce(peak[:, h % 2, 2 * c:2 * c + 2],
                                                          misc[:, c, :].rearrange("p (a b) -> p a b", a=TOK),
                                                          AX_X, ALU.max)
                        link(end)
                        nc.vector.tensor_scalar(npeak[:, h % 2, :], peak[:, h % 2, :], -(64 ** -0.5), None,
                                                ALU.mult).then_inc(npeak_ready, 1)
                    else:
                        if n >= 2:
                            dve.wait_ge(probs_turned, n - 1)
                        p = probs[:, h % 2, 0] if r < 4 else probs[:, h % 2]
                        mask = mask_a if KIND[r] == "A" else causal
                        nc.vector.scalar_tensor_tensor(
                            out=p, in0=misc[:, 0, :].rearrange("p (a b) -> p a b", a=TOK), scalar=HD ** -0.5,
                            in1=mask[:, :, :], op0=ALU.mult, op1=ALU.add).then_inc(drained[0], 1)
                        dve.wait_ge(drained[0], before[("scores", r, h)][0] + 1)
                        link(nc.vector.tensor_reduce(peak[:, h % 2, 0:2], p, AX_X, ALU.max))
                        nc.vector.tensor_scalar(npeak[:, h % 2, 0:2], peak[:, h % 2, 0:2], -1.0, None,
                                                ALU.mult).then_inc(npeak_ready, 1)
                if KIND[r] != "B" and 3 <= s < 7:
                    h = s - 3
                    dve.wait_ge(yhi_done, HEAD0[r] + h + 1 - (12 if r > 5 else 0))
                    if r < 4:
                        slot = r % Y_SLOTS
                        end = minus_hi(yt_lo[:, slot, h, :], misc[:, 3, 0:S], yt_hi[:, slot, h, :])
                    else:
                        c = 4 * (r - 6) + h
                        end = minus_hi(mt_o_lo[:, c, :], misc[:, 3, 0:S], mt_o_hi[:, c, :])
                    end.then_inc(drained[3], 1)
                if KIND[r] == "B" and s == 6:
                    dve.wait_ge(ysq_done, r - 1)
                    link(nc.vector.tensor_reduce(
                        hvar[:, :], probs1[:, 0].rearrange("p c a b -> p (c a b)").rearrange("p (h d) -> p h d", d=HD),
                        AX_X, ALU.add))
                    nc.vector.tensor_scalar(hvar[:, :], hvar[:, :], 1.0 / HD, 1e-5, ALU.mult,
                                            ALU.add).then_inc(hvar_ready, 1)
                    dve.wait_ge(hsd_ready, r - 1)
                    link(nc.vector.reciprocal(hrs[:, :], hsd[:, :]))
                    yv = ybuf[:, :, :].rearrange("p a (h d) -> p (a h) d", d=HD)
                    nc.vector.tensor_tensor(yv, yv, hrs[:, :].unsqueeze(2).to_broadcast([P, 8, HD]),
                                            ALU.mult).then_inc(y_normed, 1)
                if KIND[r] == "B" and s == 7:
                    slot = r % Y_SLOTS
                    for b in range(2):
                        dve.wait_ge(out_hi_done, 2 * (r - 2) + b + 1)
                        minus_hi(yt_lo[:, slot, 2 * b:2 * b + 2, :],
                                 misc[:, 2 + b, :].rearrange("p (a b) -> p a b", a=2),
                                 yt_hi[:, slot, 2 * b:2 * b + 2, :], sub8[:, 0:1]).then_inc(drained[2 + b], 1)

        def projections(t):
            for r in range(8):
                for j in range(2):
                    if t == ROUND_T[r] + 4 * j + 3:
                        rope(r, j)
                    if t == ROUND_T[r] + 4 * j + 4:
                        dve.wait_ge(stage_turned, 2 * r + j + 1)
                        dst = (qt1, kt1)[j] if r < 4 else (qt2, kt2)[j]
                        nc.vector.tensor_copy(dst[:, 2:4, :],
                                              misc[:, 1, :].rearrange("p (a b) -> p a b", a=2)).then_inc(drained[1], 1)

        def residual(t):
            for i in range(4):
                n = t - DOWN_T[i]
                if 0 <= n < 4:
                    g = DOWN_G[i] + n
                    add_group(t, g % 2, n)
            n = t - (FFN2_T - 4)
            if 0 <= n < 4:
                add_group(t, n % 2, n)

        def pieces(t):
            attention(t)
            projections(t)
            residual(t)
            for phase, t_last in ((1, DOWN_T[3]), (3, FFN2_T - 4)):
                if 1 <= t - t_last < 5:
                    xt_lo_piece(phase, t - t_last - 1)

        for t in range(LEAD):
            split(t, t)
        dve.wait_ge(gains_loaded, 16)
        for q in range(Q):
            xt_lo_piece(0, q)
        link(nc.vector.tensor_scalar(sub8[:, :], gains[:, G_SUBLN:G_SUBLN + 1], 1.0 - LAM_INIT, None, ALU.mult))
        link(nc.vector.tensor_tensor(gain2[:, :], gains[:, G_FINAL:G_FINAL + KD], gains[:, G_ATTN2:G_ATTN2 + KD],
                                     ALU.mult))
        variance(0)
        inverse(0)
        dve.wait_ge(lam_loaded, 16)
        dve.wait_ge(tables_loaded, 16 * 5)
        link(nc.vector.tensor_tensor(lq[:, 0:4:2, :], lq[:, 0:4:2, :], lq[:, 1:4:2, :], ALU.mult))
        nc.vector.tensor_reduce(lams[:, 0:2], lq[:, 0:4:2, :], AX_X, ALU.add).then_inc(lam_sums_ready, 1)
        dve.wait_ge(lam_exp_done, 1)
        link(nc.vector.tensor_tensor(nlam[:, :], lams[:, 3:4], lams[:, 2:3], ALU.subtract))
        link(nc.vector.tensor_scalar(nlam[:, :], nlam[:, :], -LAM_INIT, None, ALU.add))

        for t in range(FFN1_T):
            split(t + LEAD, t + LEAD)
            pieces(t)

        def gated(i, t, use):
            dve.wait_ge(pair_read[0], use + 1)
            if not isinstance(i, int):
                dve.wait_ge(hid_turned, i)
            dve.wait_ge(tile_used, t + 1)
            for tok in range(TOK):
                end = nc.vector.scalar_tensor_tensor(out=hid[:, tok, :], in0=acc[:, 1, tok, :],
                                                     scalar=rstd[:, 1, tok:tok + 1], in1=gate[:, tok, :],
                                                     op0=ALU.mult, op1=ALU.mult)
            end.then_inc(pair_read[1], 1)

        def hid_lo(i):
            for b in range(2):
                dve.wait_ge(hid_hi_done, i * 2 + b + 1)
                minus_hi(ht_lo[:, 2 * b:2 * b + 2, :], misc[:, b, :].rearrange("p (a b) -> p a b", a=2),
                         ht_hi[:, 2 * b:2 * b + 2, :]).then_inc(drained[b], 1)

        for k in range(8):
            t = FFN1_T + k
            split(t + LEAD, k + LEAD)
            if k == 0:
                pieces(t)
            if k == 1:
                variance(1)
                inverse(1)
            if k == 7:
                gated(0, t, FFN1_G // 2)
        hid_lo(0)
        with dve.Fori(1, NF) as i:
            t = i * 12 + (FFN1_T - 4)
            for k in range(12):
                split(t + k + LEAD, k + LEAD)
                if k == 7:
                    gated(i, t + k, i * 3 + (FFN1_G // 2 - 2))
                if k >= 8:
                    add_group(t + k, k % 2, k - 8)
                if k == 11:
                    hid_lo(i)
        for k in range(4):
            t = ROUND_T[4] - 4 + k
            split(t + LEAD, k + LEAD)
            add_group(t, k % 2, k)
            if k > 0:
                xt_lo_piece(2, k - 1)

        for t in range(ROUND_T[4], MERGE_T):
            split(t + LEAD, t + LEAD)
            if t == ROUND_T[4]:
                xt_lo_piece(2, 3)
                variance(2)
                inverse(2)
            if t == ROUND_T[4] + 1:
                dve.wait_ge(rstd_ready, 3)
                dve.wait_ge(row_loaded, 16)
                dve.wait_ge(tables2_loaded, 16 * 3)
                for tok in range(TOK):
                    nc.vector.scalar_tensor_tensor(out=x[:, tok, :], in0=x[:, tok, :], scalar=rstd[:, 2, tok:tok + 1],
                                                   in1=final_row[:, :], op0=ALU.mult,
                                                   op1=ALU.mult).then_inc(x1_ready, 1)
            if t == ROUND_T[4] + 2:
                variance(3)
                inverse(3)
            pieces(t)

        def merge_pieces(n, t, k, use):
            if k == 9:
                dve.wait_ge(pair_read[0], use + 1)
                dve.wait_ge(tile_used, t + 1)
                for tok in range(TOK):
                    end = nc.vector.tensor_tensor(sig_ret[:, tok, :], acc[:, 0, tok, :], sig_ret[:, tok, :], ALU.mult)
                end.then_inc(pair_read[0], 1)
            if k == 11:
                dve.wait_ge(pair_read[1], use + 1)
                dve.wait_ge(tile_used, t + 1)
                for tok in range(TOK):
                    end = nc.vector.tensor_tensor(sig_moba[:, tok, :], acc[:, 1, tok, :], sig_moba[:, tok, :],
                                                  ALU.mult)
                end.then_inc(pair_read[1], 1)
                dve.wait_ge(pair_read[1], use + 2)
                nc.vector.tensor_tensor(sig_moba[:], sig_moba[:], sig_ret[:], ALU.add).then_inc(merged_ready, 1)

        def merged_lo(n):
            for b in range(2):
                dve.wait_ge(merged_hi_done, n * 2 + b + 1)
                minus_hi(mg_lo[:, 2 * b:2 * b + 2, :], misc[:, b, :].rearrange("p (a b) -> p a b", a=2),
                         mg_hi[:, 2 * b:2 * b + 2, :]).then_inc(drained[b], 1)

        for k in range(12):
            t = MERGE_T + k
            split(t + LEAD, k + LEAD)
            merge_pieces(0, t, k, MERGE_G // 2)
            pieces(t)
        merged_lo(0)
        with dve.Fori(1, Q) as n:
            t = n * 16 + (MERGE_T - 4)
            for k in range(16):
                split(t + k + LEAD, k + LEAD)
                merge_pieces(n, t + k, k, n * 4 + (MERGE_G // 2 - 2))
                if k >= 12:
                    add_group(t + k, k % 2, k - 12)
                if k == 15:
                    merged_lo(n)
        for k in range(4):
            t = FFN2_T - 4 + k
            split(t + LEAD, k + LEAD)
            pieces(t)

        def taps_on(i, half, dst):
            for w, gone in ((1, 1), (0, 2)):
                for j in range(C):
                    if j % 2 == 0:
                        if w == 1:
                            dve.wait_ge(tap2_done, i * 4 + (2 * half + j // 2 + 1))
                        else:
                            dve.wait_ge(tap1_done, i * 4 + (2 * half + j // 2 + 1))
                    col = i * C + (half * FF // P + j)
                    src = misc[:, 2 * half + j // 2, (j % 2) * S:(j % 2 + 1) * S - gone]
                    end = nc.vector.scalar_tensor_tensor(out=dst[:, j, gone:], in0=src,
                                                         scalar=taps[:, w, bass.ds(col, 1)], in1=dst[:, j, gone:],
                                                         op0=ALU.mult, op1=ALU.add)
                    if w == 1 and j % 2:
                        end.then_inc(tap1_done, 1)
                    if w == 0 and j % 2:
                        end.then_inc(drained[2 * half + j // 2], 1)

        def product(i):
            dve.wait_ge(silu_done, i + 1)
            dve.wait_ge(drained[3], i + (before[("ffn2b", 0)][3] + 1))
            nc.vector.tensor_tensor(conv_a[:], conv_a[:], conv_b[:], ALU.mult).then_inc(prod_done, 1)

        def product_lo(i):
            dve.wait_ge(h2_hi_done, i + 1)
            nc.vector.tensor_tensor(h2_lo[:], conv_a[:], h2_hi[:].bitcast(F32), ALU.subtract).then_inc(h2_ready, 1)

        for k in range(8):
            t = FFN2_T + k
            split(t + LEAD, k + LEAD)
            if k == 0:
                pieces(t)
            if k == 1:
                variance(4)
                inverse(4)
            if k == 5:
                taps_on(0, 0, conv_a)
            if k == 7:
                taps_on(0, 1, conv_b)
                product(0)
                product_lo(0)
        with dve.Fori(1, NF) as i:
            t = i * 12 + (FFN2_T - 4)
            for k in range(12):
                split(t + k + LEAD, k + LEAD)
                if k == 5:
                    taps_on(i, 0, conv_a)
                if k == 9:
                    taps_on(i, 1, conv_b)
                if k == 10:
                    product(i)
                if k >= 8:
                    add_group(t + k, k % 2, k - 8)
                if k == 11:
                    product_lo(i)
        for k in range(4):
            t = TILES - 4 + k
            split(t + LEAD, k + LEAD)
            add_group(t, k % 2, k)
        variance(5)
        inverse(5)
        dve.wait_ge(rstd_ready, 6)
        dve.wait_ge(row_loaded, 32)
        for tok in range(TOK):
            nc.vector.scalar_tensor_tensor(out=x[:, tok, :], in0=x[:, tok, :], scalar=rstd[:, 5, tok:tok + 1],
                                           in1=final_row[:, :], op0=ALU.mult, op1=ALU.mult).then_inc(out_ready, 1)

    ctx.close()


def tables():
    f32 = np.float32
    i = np.arange(S)
    by_tile = lambda a: np.ascontiguousarray(a.reshape(TOK, P, -1).transpose(1, 0, 2))
    times = np.zeros((S, S), f32)
    for window, dil in ((128, 1), (512, 4), (2048, 16)):
        gap = np.abs(i[:, None] - i[None, :])
        times += (gap % dil == 0) & (gap // dil <= window // (2 * dil))
    off = lambda allowed: np.where(allowed, 0.0, NEG).astype(f32)

    def rope(rot, theta):
        inv = (f32(theta) ** (-np.arange(0, rot, 2, dtype=f32) / f32(rot))).astype(f32)
        ang = i.astype(f32)[:, None] * inv[None, :]
        cos, sin = (f(ang.astype(np.float64)).astype(f32) for f in (np.cos, np.sin))
        return np.stack([by_tile(np.concatenate([cos, cos], 1)), by_tile(np.concatenate([-sin, sin], 1))], 1)

    decay = np.zeros((P, 4, 384), f32)
    for h in range(4):
        log_g = np.log1p(-(2.0 ** (-5.0 - h)))
        dist = i[None, :] - i[:, None]
        full = np.where(dist >= 0, np.exp(log_g * np.maximum(dist, 0)), 0.0) * RD ** -0.5
        decay[:, h, :S] = full[:P]
        decay[:, h, S:] = full[P:, P:]
    return {
        "ident": np.eye(P, dtype=f32), "mask_a": by_tile(off(times > 0)), "mult_a": by_tile(times),
        "causal": by_tile(off(i[None, :] <= i[:, None])), "decay": decay,
        "rope_a": rope(32, 500000.0), "rope_b": rope(16, 500000.0), "rope_r": rope(RD, 10000.0),
    }


NAMES = ["x", "w_in", "lambda_qk", "w_out", "w_gate", "w_up", "w_down", "norm_final", "w_in_2", "w_ret_up_2",
         "w_moba_up_2", "w_out_2", "w_ffn_up_2", "w_ffn_down_2", "final_norm_w_2"]


def kernel(**inputs):
    from concourse import bacc
    from concourse.bass_utils import run_bass_kernel_spmd

    arrays = {n: np.ascontiguousarray(inputs[n]) for n in NAMES}
    arrays.update(tables())
    rows = [inputs[n].reshape(-1, P) for n in
            ("norm_attn", "norm_ffn", "attn_norm_w_2", "ffn_norm_w_2", "norm_final", "ret_norm_w_2", "subln")]
    arrays["gains"] = np.ascontiguousarray(np.concatenate(rows, 0).T)
    taps = np.concatenate([inputs["conv_w_2"][0], inputs["conv_b_2"]], 0)
    arrays["taps"] = np.ascontiguousarray(taps.reshape(4, -1, P).transpose(2, 0, 1))

    nc = bacc.Bacc("TRN2", target_bir_lowering=False, num_devices=1)
    ins = {n: nc.dram_tensor(f"in_{n}", a.shape, mybir.dt.from_np(a.dtype), kind="ExternalInput").ap()
           for n, a in arrays.items()}
    out = nc.dram_tensor("out", (1, S, D), F32, kind="ExternalOutput").ap()
    build(nc, ins, out)
    r = run_bass_kernel_spmd(nc, [{f"in_{n}": a for n, a in arrays.items()}], core_ids=[0])
    return r.results[0]["out"]
```

```python
from contextlib import ExitStack

import numpy as np

import concourse.bass as bass
from concourse import mybir
from concourse.alu_op_type import AluOpType as ALU

F32 = mybir.dt.float32
F32R = mybir.dt.float32r
ACT = mybir.ActivationFunctionType
AX_X = mybir.AxisListType.X

P = 128
S = 256
TOK = S // P
D = 2048
KD = D // P
N = 512
C = 4
Q = D // N
FF = 5632
NF = FF // N
HD = 128
RD = 256
RING = 4
LEAD = RING - 1
NEG = -1e30
LAM_INIT = 0.8 - 0.6 * 1.0

KIND = "AABBRRMM"
HEADS = [2 if k == "R" else 4 for k in KIND]
HEAD0 = [sum(HEADS[:r]) for r in range(len(KIND))]

ROUND_T = [0, 12, 28, 40, 196, 212, 228, 240]
DOWN_T = [24, 52, 56, 60]
FFN1_T = 64
MERGE_T = 252
FFN2_T = 316
TILES = 448
TURN = (6, 9)
WINDOW = [12, 24, 40, 50, 208, 224, 240, 252]
ROUND_G = [0, 3, 10, 13, 94, 98, 102, 105]
DOWN_G = [6, 16, 20, 24]
FFN1_G = 28
MERGE_G = 108
FFN2_G = 140
LAST_G = FFN2_G + 6 * NF - 4
assert FFN1_T + 4 * 3 * NF == ROUND_T[4] and FFN2_T + 4 * 3 * NF == TILES

WARM_UP = 14
Y_SLOTS = 3

G_ATTN1, G_FFN1, G_ATTN2, G_FFN2, G_FINAL, G_RET, G_SUBLN = 0, 16, 32, 48, 64, 80, 88
N_GAINS = 89


def keys_of(kind, qt):
    return (qt + 1) * P if kind == "M" else S


def plan_misc_banks():
    used = [0] * 4
    before = {}

    def piece(key, banks):
        before[key] = {b: used[b] for b in banks}
        for b in banks:
            used[b] += 1

    def xt(phase, q):
        piece(("xt", phase, q), (0, 1) if q % 2 == 0 else (2, 3))

    def attention(r, s):
        if KIND[r] == "R":
            if 0 <= s < 2:
                piece(("scores", r, s), (s,))
            if 1 <= s < 3:
                piece(("values", r, s - 1), (s + 1,))
            if s == 5:
                piece(("out", r), (2, 3))
            return
        if 2 <= s < 6:
            piece(("probs", r, s - 2), (2,))
        if 0 <= s < 4:
            piece(("scores", r, s), (0, 1) if KIND[r] == "B" else (0,))
        if 3 <= s < 7:
            piece(("values", r, s - 3), (3,))
        if KIND[r] == "B" and s == 8:
            piece(("out", r), (2, 3))

    def steps(t0, t1):
        for t in range(t0, t1):
            for r in range(8):
                attention(r, t - WINDOW[r])
                if t - ROUND_T[r] in TURN:
                    piece(("turn", r, TURN.index(t - ROUND_T[r])), (0, 1))
            for phase, t_last in ((1, DOWN_T[3]), (3, MERGE_T + 60)):
                if 1 <= t - t_last < 5:
                    xt(phase, t - t_last - 1)

    for q in range(Q):
        xt(0, q)
    steps(0, FFN1_T + 1)
    for i in range(NF):
        piece(("ffn1", i), (0, 1))
        if i == 0:
            first = dict(before[("ffn1", 0)])
    assert before[("ffn1", NF - 1)] == {b: first[b] + NF - 1 for b in first}
    for q in range(3):
        xt(2, q)
    xt(2, 3)
    steps(ROUND_T[4], MERGE_T + 12)
    for n in range(Q):
        piece(("merge", n), (0, 1))
    steps(MERGE_T + 12, FFN2_T + 1)
    for i in range(NF):
        piece(("ffn2a", i), (0, 1))
        piece(("ffn2b", i), (2, 3))
    return before


def build(nc, ins, out):
    ctx = ExitStack()
    base = 16512

    def place(name, shape, dtype, at):
        return nc.alloc_sbuf_tensor_at(name, shape, dtype, offset=at)

    KB = 1024
    raw = place("w_raw", [P, RING, C, N], F32, base)
    w_hi = place("w_hi", [P, RING, C, N], F32R, base + 32 * KB)
    w_lo = place("w_lo", [P, RING, C, N], F32R, base + 64 * KB)
    x = place("x", [P, TOK, D], F32, base + 96 * KB)
    xt_hi = place("xt_hi", [P, KD, S], F32R, base + 112 * KB)
    xt_lo = place("xt_lo", [P, KD, S], F32R, base + 128 * KB)
    ph = base + 144 * KB
    yt_hi = place("yt_hi", [P, Y_SLOTS, C, S], F32R, ph)
    yt_lo = place("yt_lo", [P, Y_SLOTS, C, S], F32R, ph + 12 * KB)
    shift = 8 * KB
    stage1 = place("qk_stage1", [P, TOK, N], F32, ph + 16 * KB + shift)
    qt1 = place("q_t1", [P, C, S], F32, ph + 20 * KB + shift)
    kt1 = place("k_t1", [P, C, S], F32, ph + 24 * KB + shift)
    v1 = place("v1", [P, TOK, N], F32, ph + 28 * KB + shift)
    probs1 = place("probs1", [P, 2, 2, TOK, S], F32, ph + 40 * KB)
    pt1 = place("probs_t1", [P, TOK, S], F32, ph + 48 * KB)
    ybuf = place("y", [P, TOK, N], F32, ph + 50 * KB)
    mask_a = place("mask_a", [P, TOK, S], F32, ph + 54 * KB)
    mult_a = place("mult_a", [P, TOK, S], F32, ph + 56 * KB)
    junk = place("junk", [P, N], F32, ph + 58 * KB)
    ht_hi = place("ht_hi", [P, C, S], F32R, ph)
    ht_lo = place("ht_lo", [P, C, S], F32R, ph + 4 * KB)
    ht_last_hi = place("ht_last_hi", [P, C, S], F32R, ph + 16 * KB)
    ht_last_lo = place("ht_last_lo", [P, C, S], F32R, ph + 20 * KB)
    gate = place("gate", [P, TOK, N], F32, ph + 8 * KB)
    hid = place("hid", [P, TOK, N], F32, ph + 12 * KB)
    ot_hi = place("ot_hi", [P, 8, S], F32R, ph)
    ot_lo = place("ot_lo", [P, 8, S], F32R, ph + 8 * KB)
    stage2 = place("qk_stage2", [P, TOK, N], F32, ph + 16 * KB)
    qt2 = place("q_t2", [P, C, S], F32, ph + 20 * KB)
    kt2 = place("k_t2", [P, C, S], F32, ph + 24 * KB)
    v2 = place("v2", [P, TOK, N], F32, ph + 28 * KB)
    z = ph + 32 * KB
    ret_g = place("ret_gate", [P, TOK, N], F32, z)
    ret_o = place("ret_o", [P, TOK, N], F32, z + 4 * KB)
    final_row = place("final_row", [P, D], F32, z)
    ret_s = place("ret_scores", [P, 2, 384], F32, z + 8 * KB)
    decay = place("decay", [P, 4, 384], F32, z + 11 * KB)
    rope_r = place("rope_r", [P, 2, TOK, RD], F32, z + 17 * KB)
    causal = place("causal", [P, TOK, S], F32, z + 21 * KB)
    mt_o_hi = place("moba_t_hi", [P, 8, S], F32R, z)
    mt_o_lo = place("moba_t_lo", [P, 8, S], F32R, z + 8 * KB)
    probs2 = place("probs2", [P, 2, TOK, S], F32, z + 16 * KB)
    pt2 = place("probs_t2", [P, S + P], F32, z + 23 * KB)
    sig_ret = place("sig_ret", [P, TOK, N], F32, ph + 16 * KB)
    sig_moba = place("sig_moba", [P, TOK, N], F32, ph + 20 * KB)
    mg_hi = place("merged_t_hi", [P, C, S], F32R, ph + 24 * KB)
    mg_lo = place("merged_t_lo", [P, C, S], F32R, ph + 28 * KB)
    mg_last_hi = place("merged_last_hi", [P, C, S], F32R, z + 16 * KB)
    mg_last_lo = place("merged_last_lo", [P, C, S], F32R, z + 20 * KB)
    h2_hi = place("h2_hi", [P, C, S], F32R, ph)
    h2_lo = place("h2_lo", [P, C, S], F32R, ph + 4 * KB)
    ubuf = place("u", [P, TOK, N], F32, ph + 8 * KB)
    conv_a = place("conv_a", [P, C, S], F32, ph + 12 * KB)
    conv_b = place("conv_b", [P, C, S], F32, ph + 16 * KB)
    h2_last_hi = place("h2_last_hi", [P, C, S], F32R, ph + 24 * KB)
    h2_last_lo = place("h2_last_lo", [P, C, S], F32R, ph + 28 * KB)
    at = ph + 60 * KB

    def small(name, *shape):
        nonlocal at
        t = place(name, [P, *shape], F32, at)
        at += 4 * int(np.prod(shape))
        at += -at % 32
        return t

    ident = small("ident", P)
    gains = small("gains", N_GAINS)
    taps = small("taps", 4, 2 * FF // P)
    rope_a = small("rope_a", 2, TOK, 32)
    rope_b = small("rope_b", 2, TOK, 16)
    sumsq = small("sumsq", 6, TOK, Q)
    var = small("var", 6, TOK)
    sd = small("sd", 6, TOK)
    rstd = small("rstd", 6, TOK)
    gain2 = small("gain2", KD)
    peak = small("peak", 2, 4)
    npeak = small("npeak", 2, 4)
    den = small("den", 2, 4)
    rden = small("rden", 2, 4)
    hsum = small("head_sumsq", 8)
    hvar = small("head_var", 8)
    hsd = small("head_sd", 8)
    hrs = small("head_rstd", 8)
    lams = small("lams", 4)
    nlam = small("minus_lam", 1)
    sub8 = small("subln_scaled", 1)
    assert at <= 229344
    lq = ybuf[:, 0, 0:256].rearrange("p (a b) -> p a b", a=4)

    acc = ctx.enter_context(nc.psum_tensor("acc", [P, 2, TOK, N], F32))
    misc = ctx.enter_context(nc.psum_tensor("misc", [P, 4, N], F32))

    def sem(name):
        return ctx.enter_context(nc.semaphore(name))

    raw_ready = [sem(f"raw_ready{i}") for i in range(RING)]
    hi_ready = sem("hi_ready")
    lo_ready = sem("lo_ready")
    tile_used = sem("tile_used")
    pair_read = [sem("pair0_read"), sem("pair1_read")]
    drained = [sem(f"misc{b}_drained") for b in range(4)]
    x_loaded = [sem(f"x_loaded{q}") for q in range(Q)]
    ident_loaded = sem("ident_loaded")
    gains_loaded = sem("gains_loaded")
    ropes_loaded = sem("ropes_loaded")
    tables_loaded = sem("tables_loaded")
    lam_loaded = sem("lam_loaded")
    tables2_loaded = sem("tables2_loaded")
    row_loaded = sem("final_row_loaded")
    stored = sem("stored")
    x_gained = sem("x_gained")
    out_dve_ready = sem("out_dve_ready")
    out_act_ready = sem("out_act_ready")
    xt_turned = sem("xt_turned")
    xt_hi_done = sem("xt_hi_done")
    sumsq_done = sem("sumsq_done")
    var_ready = sem("var_ready")
    sd_ready = sem("sd_ready")
    table_loaded = sem("table_loaded")
    rstd_ready = sem("rstd_ready")
    stage_roped = sem("stage_roped")
    stage_turned = sem("stage_turned")
    scores_done = sem("scores_done")
    npeak_ready = sem("npeak_ready")
    exp_done = sem("exp_done")
    rden_ready = sem("rden_ready")
    probs_ready = sem("probs_ready")
    probs_turned = sem("probs_turned")
    values_done = sem("values_done")
    yhi_done = sem("y_hi_done")
    ysq_done = sem("y_squares_done")
    hvar_ready = sem("head_var_ready")
    hsd_ready = sem("head_sd_ready")
    y_normed = sem("y_normed")
    y_turned = sem("y_turned")
    out_hi_done = sem("out_hi_done")
    hid_turned = sem("hid_turned")
    hid_hi_done = sem("hid_hi_done")
    merged_ready = sem("merged_ready")
    merged_turned = sem("merged_turned")
    merged_hi_done = sem("merged_hi_done")
    u_turned = sem("u_turned")
    tap2_done = sem("tap2_done")
    tap1_done = sem("tap1_done")
    silu_done = sem("silu_done")
    prod_done = sem("prod_done")
    h2_hi_done = sem("h2_hi_done")
    h2_ready = sem("h2_ready")
    dve_link = sem("dve_link")
    sub8_done = sem("sub8_done")
    lam_sums_ready = sem("lam_sums_ready")
    lam_exp_done = sem("lam_exp_done")

    before = plan_misc_banks()

    def slot_count(t, k):
        return (t - k % RING) * (16 // RING) + 16

    def group_read(eng, g):
        eng.wait_ge(pair_read[g % 2], g // 2 + 1)

    def x_quarter(eng, stage, q):
        group_read(eng, {1: DOWN_G[3], 2: ROUND_G[4] - 4, 4: FFN2_G - 4, 5: LAST_G}[stage] + q)

    def tile_of(w, row, col):
        return w[bass.ds(row, C * P), bass.ds(col, N)].rearrange("(c p) n -> p c n", p=P)

    QKV_COL = {"A": (0, 1024, 2048), "B": (3072, 4096, 5120),
               "R": (0, 1024, 2048, 3072), "M": (4096, 5120, 6144)}
    GR_COL, GM_COL = 7168, 9216

    def part(r):
        return r % 2

    block = ctx.enter_context(nc.Block())

    @block.sync
    def _(sp):
        xr = ins["x"].rearrange("b (a p) d -> p (b a) d", p=P)
        sp.dma_start(ident[:, :], ins["ident"]).then_inc(ident_loaded, 16)
        sp.dma_start(gains[:, :], ins["gains"]).then_inc(gains_loaded, 16)

        def load_x(q):
            sp.dma_start(x[:, :, q * N:(q + 1) * N], xr[:, :, q * N:(q + 1) * N]).then_inc(x_loaded[q], 16)

        def load(t, k, src):
            if isinstance(t, int) and t < RING:
                load_x(t)
            else:
                sp.wait_ge(lo_ready, t - RING + 1)
            sp.dma_start(raw[:, k % RING], src).then_inc(raw_ready[k % RING], 16)

        def project(t0, w, cols):
            for g, col in enumerate(cols):
                for j in range(Q):
                    load(t0 + 4 * g + j, j, tile_of(w, j * C * P, col))

        def down(t0, w, row):
            for n in range(Q):
                load(t0 + n, n, tile_of(w, row, n * N))

        w_in, w_out = ins["w_in"][0], ins["w_out"][0]
        for r in range(4):
            project(ROUND_T[r], w_in, [c + part(r) * N for c in QKV_COL[KIND[r]]])
            if r == 1:
                down(DOWN_T[0], w_out, 0)
        for i in range(1, 4):
            down(DOWN_T[i], w_out, i * N)

        w_gate, w_up, w_down = ins["w_gate"][0], ins["w_up"][0], ins["w_down"][0]
        project(FFN1_T, w_gate, [0])
        project(FFN1_T + 4, w_up, [0])
        with sp.Fori(1, NF) as i:
            t = i * 12 + (FFN1_T - 4)
            project(t, w_gate, [i * N])
            project(t + 4, w_up, [i * N])
            down(t + 8, w_down, i * N - N)
        down(ROUND_T[4] - 4, w_down, (NF - 1) * N)

        w_in2 = ins["w_in_2"][0]
        for r in range(4, 8):
            project(ROUND_T[r], w_in2, [c + part(r) * N for c in QKV_COL[KIND[r]]])

        def merge_loads(t, n):
            project(t, w_in2, [n * N + GR_COL])
            project(t + 4, w_in2, [n * N + GM_COL])
            for j in range(2):
                load(t + 8 + j, j, tile_of(ins["w_ret_up_2"][0], j * C * P, n * N))
            for j in range(2):
                load(t + 10 + j, 2 + j, tile_of(ins["w_moba_up_2"][0], j * C * P, n * N))

        merge_loads(MERGE_T, 0)
        for n in range(1, Q):
            t = n * 16 + (MERGE_T - 4)
            merge_loads(t, n)
            down(t + 12, ins["w_out_2"][0], n * N - N)
        down(FFN2_T - 4, ins["w_out_2"][0], (Q - 1) * N)

        w_up2, w_down2 = ins["w_ffn_up_2"][0], ins["w_ffn_down_2"][0]
        project(FFN2_T, w_up2, [0])
        project(FFN2_T + 4, w_up2, [FF])
        with sp.Fori(1, NF) as i:
            t = i * 12 + (FFN2_T - 4)
            project(t, w_up2, [i * N])
            project(t + 4, w_up2, [i * N + FF])
            down(t + 8, w_down2, i * N - N)
        down(TILES - 4, w_down2, (NF - 1) * N)

        orr = out.rearrange("b (a p) d -> a p (b d)", p=P)
        for half in range(2):
            cols = slice(half * D // 2, (half + 1) * D // 2)
            for tok in range(TOK):
                if tok == 0:
                    sp.wait_ge(out_dve_ready, half + 1)
                else:
                    sp.wait_ge(out_act_ready, half + 1)
                    if half == 1:
                        sp.wait_ge(out_dve_ready, 3)
                sp.dma_start(orr[tok][:, cols], x[:, tok, cols]).then_inc(stored, 16)
        sp.wait_ge(stored, 16 * 2 * TOK)

    @block.gpsimd
    def _(pool):
        def load(dst, src, signal):
            pool.dma_start(dst, src).then_inc(signal, 16)

        load(rope_a[:], ins["rope_a"], ropes_loaded)
        load(rope_b[:], ins["rope_b"], ropes_loaded)
        load(lq, ins["lambda_qk"].partition_broadcast(P)[:, 0], lam_loaded)
        pool.wait_ge(tile_used, 1)
        load(mask_a[:], ins["mask_a"], tables_loaded)
        load(mult_a[:], ins["mult_a"], tables_loaded)
        load(taps[:], ins["taps"], tables_loaded)
        pool.wait_ge(tile_used, FFN1_T + 1)
        load(final_row[:], ins["norm_final"].partition_broadcast(P), row_loaded)
        load(decay[:], ins["decay"], tables2_loaded)
        load(rope_r[:], ins["rope_r"], tables2_loaded)
        load(causal[:], ins["causal"], tables2_loaded)
        pool.wait_ge(tile_used, FFN2_T + 1)
        load(final_row[:], ins["final_norm_w_2"].partition_broadcast(P), row_loaded)

    @block.tensor
    def _(pe):
        def products(t, k, pair, a_hi, a_lo, first=True, last=True):
            pe.wait_ge(lo_ready, t + 1)
            for tok in range(TOK):
                for j in range(C):
                    hi = a_hi[:, j, tok * P:(tok + 1) * P]
                    lo = a_lo[:, j, tok * P:(tok + 1) * P]
                    bank = acc[:, pair, tok, :]
                    nc.tensor.matmul(bank, hi, w_hi[:, k % RING, j, :], start=first and j == 0, stop=False)
                    nc.tensor.matmul(bank, hi, w_lo[:, k % RING, j, :], start=False, stop=False)
                    end = nc.tensor.matmul(bank, lo, w_hi[:, k % RING, j, :], start=False,
                                           stop=last and j == C - 1)
            end.then_inc(tile_used, 1)

        def pair_free(pair, use):
            if isinstance(use, int) and use == 0:
                return
            pe.wait_ge(pair_read[pair], use)

        def bank_free(b, use):
            if isinstance(use, int) and use == 0:
                return
            pe.wait_ge(drained[b], use)

        def banks_free(key):
            for b, use in before[key].items():
                bank_free(b, use)

        def turn(src, banks):
            for j in range(C):
                for tok in range(TOK):
                    end = nc.tensor.transpose(
                        misc[:, banks[j // 2], (j % 2) * S + tok * P:(j % 2) * S + (tok + 1) * P],
                        src[:, tok, j * P:(j + 1) * P], ident[:, :])
            return end

        def xt_piece(phase, q):
            if phase == 0:
                pe.wait_ge(x_loaded[q], 16)
            else:
                x_quarter(pe, {1: 1, 2: 2, 3: 4}[phase], q)
            banks_free(("xt", phase, q))
            banks = (0, 1) if q % 2 == 0 else (2, 3)
            turn(x[:, :, q * N:(q + 1) * N], banks).then_inc(xt_turned, 1)

        def xt_ready(phase, q):
            for b, use in before[("xt", phase, q)].items():
                pe.wait_ge(drained[b], use + 1)

        def attention(t):
            for r in range(8):
                s = t - WINDOW[r]
                q_t, k_t, v, probs, p_t = (qt1, kt1, v1, probs1, pt1) if r < 4 else (qt2, kt2, v2, probs2, pt2)
                if KIND[r] == "R":
                    if 0 <= s < 2:
                        h = s
                        if h == 0:
                            for j in range(2):
                                for b in (0, 1):
                                    pe.wait_ge(drained[b], before[("turn", r, j)][b] + 1)
                        banks_free(("scores", r, h))
                        for kt in range(TOK):
                            for dc in range(2):
                                end = nc.tensor.matmul(
                                    misc[:, h, kt * S:(kt + 1) * S - kt * P],
                                    k_t[:, 2 * h + dc, kt * P:(kt + 1) * P], q_t[:, 2 * h + dc, kt * P:],
                                    start=dc == 0, stop=dc == 1)
                        end.then_inc(scores_done, 1)
                    if 1 <= s < 3:
                        h = s - 1
                        if h == 0:
                            group_read(pe, ROUND_G[r] + 2)
                        pe.wait_ge(drained[h], before[("scores", r, h)][h] + 1)
                        banks_free(("values", r, h))
                        vh = v[:, :, h * RD:(h + 1) * RD]
                        nc.tensor.matmul(misc[:, 2 + h, 0:RD], ret_s[:, h, 0:P], vh[:, 0, :], start=True, stop=True)
                        nc.tensor.matmul(misc[:, 2 + h, RD:], ret_s[:, h, P:S], vh[:, 0, :], start=True, stop=False)
                        nc.tensor.matmul(misc[:, 2 + h, RD:], ret_s[:, h, S:], vh[:, 1, :], start=False,
                                         stop=True).then_inc(values_done, 1)
                    if s == 5:
                        pe.wait_ge(y_normed, r - 1)
                        banks_free(("out", r))
                        turn(ret_o, (2, 3)).then_inc(y_turned, 1)
                    continue
                if 2 <= s < 6:
                    h = s - 2
                    pe.wait_ge(probs_ready, HEAD0[r] + h + 1 - (4 if r > 5 else 0))
                    banks_free(("probs", r, h))
                    src = probs[:, h % 2, 0] if r < 4 else probs[:, h % 2]
                    for kt in range(TOK):
                        for qt in range(TOK):
                            if kt * P >= keys_of(KIND[r], qt):
                                continue
                            at = kt * S + (qt - kt if KIND[r] == "M" else qt) * P
                            end = nc.tensor.transpose(misc[:, 2, at:at + P], src[:, qt, kt * P:(kt + 1) * P],
                                                      ident[:, :])
                    end.then_inc(probs_turned, 1)
                if 0 <= s < 4:
                    h = s
                    if h == 0:
                        for j in range(2):
                            for b in (0, 1):
                                pe.wait_ge(drained[b], before[("turn", r, j)][b] + 1)
                    banks_free(("scores", r, h))
                    if KIND[r] == "B":
                        for c in range(2):
                            rows = slice(c * 64, (c + 1) * 64)
                            for qt in range(TOK):
                                end = nc.tensor.matmul(misc[:, c, qt * S:(qt + 1) * S],
                                                       q_t[rows, h, qt * P:(qt + 1) * P], k_t[rows, h, :],
                                                       start=True, stop=True)
                    else:
                        for qt in range(TOK):
                            keys = keys_of(KIND[r], qt)
                            end = nc.tensor.matmul(misc[:, 0, qt * S:qt * S + keys],
                                                   q_t[:, h, qt * P:(qt + 1) * P], k_t[:, h, 0:keys],
                                                   start=True, stop=True)
                    end.then_inc(scores_done, 1)
                if 3 <= s < 7:
                    h = s - 3
                    if h == 0:
                        group_read(pe, ROUND_G[r] + 2)
                    pe.wait_ge(drained[2], before[("probs", r, h)][2] + 1)
                    banks_free(("values", r, h))
                    if KIND[r] == "M":
                        vh = v[:, :, h * HD:(h + 1) * HD]
                        nc.tensor.matmul(misc[:, 3, 0:P], vh[:, 0, :], pt2[:, 0:P], start=True, stop=True)
                        nc.tensor.matmul(misc[:, 3, P:S], vh[:, 0, :], pt2[:, P:S], start=True, stop=False)
                        end = nc.tensor.matmul(misc[:, 3, P:S], vh[:, 1, :], pt2[:, S:], start=False, stop=True)
                    elif KIND[r] == "A":
                        for kt in range(TOK):
                            end = nc.tensor.matmul(misc[:, 3, 0:S], v[:, kt, h * HD:(h + 1) * HD], p_t[:, kt, :],
                                                   start=kt == 0, stop=kt == 1)
                    else:
                        for qt in range(TOK):
                            for kt in range(TOK):
                                end = nc.tensor.matmul(misc[:, 3, qt * HD:(qt + 1) * HD],
                                                       p_t[:, kt, qt * P:(qt + 1) * P],
                                                       v[:, kt, h * HD:(h + 1) * HD],
                                                       start=kt == 0, stop=kt == 1)
                    end.then_inc(values_done, 1)
                if KIND[r] == "B" and s == 8:
                    pe.wait_ge(y_normed, r - 1)
                    banks_free(("out", r))
                    turn(ybuf, (2, 3)).then_inc(y_turned, 1)

        def stage_turn(t):
            for r in range(8):
                if t - ROUND_T[r] in TURN:
                    j = TURN.index(t - ROUND_T[r])
                    n = 2 * r + j
                    pe.wait_ge(stage_roped, n + 1)
                    banks_free(("turn", r, j))
                    turn(stage1 if r < 4 else stage2, (0, 1)).then_inc(stage_turned, 1)

        def small_pieces(t):
            attention(t)
            stage_turn(t)
            if t in (0, 1):
                xt_piece(0, t + 2)
            for phase, t_last in ((1, DOWN_T[3]), (3, FFN2_T - 4)):
                if 1 <= t - t_last < 5:
                    xt_piece(phase, t - t_last - 1)

        def project(t0, pair, use, phase=None, a=(xt_hi, xt_lo), tiles=Q, after=None, wait=None, k0=0):
            pair_free(pair, use)
            if wait:
                wait()
            for j in range(tiles):
                if phase is not None:
                    xt_ready(phase, j)
                products(t0 + j, k0 + j, pair, a[0][:, C * j:C * (j + 1)], a[1][:, C * j:C * (j + 1)],
                         first=j == 0, last=j == tiles - 1)
                if after:
                    after(t0 + j)

        def down(t0, pair0, use0, a_hi, a_lo, after=None):
            for n in range(Q):
                pair = (pair0 + n) % 2
                pair_free(pair, use0 + (pair0 + n) // 2)
                products(t0 + n, n, pair, a_hi, a_lo)
                if after:
                    after(t0 + n)

        def at_first(piece):
            seen = []

            def after(t):
                if not seen:
                    piece()
                seen.append(t)
            return after

        pe.wait_ge(ident_loaded, 16)
        for q in range(2):
            xt_piece(0, q)
        for _ in range(WARM_UP):
            nc.tensor.transpose(acc[:, 0, 0, 0:P], ident[:, :], ident[:, :])

        def block_round(r, phase, groups):
            for g in range(groups):
                n = ROUND_G[r] + g
                project(ROUND_T[r] + 4 * g, n % 2, n // 2, phase if g == 0 else None, after=small_pieces)

        def y_ready(i):
            if KIND[i] == "B":
                for b in (2, 3):
                    pe.wait_ge(drained[b], before[("out", i)][b] + 1)
            else:
                pe.wait_ge(drained[3], before[("values", i, 3)][3] + 1)

        def block_down(i):
            y_ready(i)
            s = i % Y_SLOTS
            down(DOWN_T[i], DOWN_G[i] % 2, DOWN_G[i] // 2, yt_hi[:, s], yt_lo[:, s], after=small_pieces)

        for r in range(4):
            block_round(r, 0 if r == 0 else None, 3)
            if r == 1:
                block_down(0)
        for i in range(1, 4):
            block_down(i)

        def hid_turn(i, use):
            pe.wait_ge(pair_read[1], use + 1)
            for b in (0, 1):
                bank_free(b, before[("ffn1", 0)][b] + i)
            turn(hid, (0, 1)).then_inc(hid_turned, 1)

        def ffn1_down(t, use, i, after=None, a=(ht_hi, ht_lo)):
            for b in (0, 1):
                pe.wait_ge(drained[b], before[("ffn1", 0)][b] + i + 1)
            down(t, 0, use, *a, after)

        def ffn1(i):
            t = i * 12 + (FFN1_T - 4)
            use = i * 3 + (g - 2)
            first = isinstance(i, int)
            project(t, 0, use, after=at_first(lambda: hid_turn(0, g)) if first else None)
            project(t + 4, 1, use)
            ffn1_down(t + 8, use + 1, i - 1, after=at_first(lambda: hid_turn(i, use)))

        g = FFN1_G // 2
        project(FFN1_T, 0, g, 1, after=small_pieces)
        project(FFN1_T + 4, 1, g)
        ffn1(1)
        with pe.Fori(2, NF) as i:
            ffn1(i)
        ffn1_down(ROUND_T[4] - 4, g - 2 + 3 * NF, NF - 1, a=(ht_last_hi, ht_last_lo),
                  after=lambda t: xt_piece(2, t - ROUND_T[4] + 3) if t > ROUND_T[4] - 4 else None)

        for r in range(4, 8):
            for gi in range(HEADS[r] == 2 and 4 or 3):
                n = ROUND_G[r] + gi

                def after(t):
                    if t == ROUND_T[4]:
                        xt_piece(2, 3)
                    small_pieces(t)

                project(ROUND_T[r] + 4 * gi, n % 2, n // 2, 2 if (r == 4 and gi == 0) else None, after=after)

        def ret_ready():
            for r in (4, 5):
                for b in (2, 3):
                    pe.wait_ge(drained[b], before[("out", r)][b] + 1)

        def moba_ready():
            pe.wait_ge(drained[3], before[("values", 7, 3)][3] + 1)

        def merge(t, use, peeled, first=None):
            after = small_pieces if peeled else None
            project(t, 0, use, after=first or after)
            project(t + 4, 1, use, after=after)
            project(t + 8, 0, use + 1, a=(ot_hi, ot_lo), tiles=2, after=after, wait=ret_ready if peeled else None)
            project(t + 10, 1, use + 1, a=(mt_o_hi, mt_o_lo), tiles=2, after=after,
                    wait=moba_ready if peeled else None, k0=2)

        def merged_turn(n):
            pe.wait_ge(merged_ready, n + 1)
            for b in (0, 1):
                bank_free(b, before[("merge", 0)][b] + n)
            turn(sig_moba, (0, 1)).then_inc(merged_turned, 1)

        def merge_down(t, use, n, after=None, a=(mg_hi, mg_lo)):
            for b in (0, 1):
                pe.wait_ge(drained[b], before[("merge", 0)][b] + n + 1)
            down(t, 0, use, *a, after)

        def merge_slice(n):
            t = n * 16 + (MERGE_T - 4)
            use = n * 4 + (g - 2)
            merge(t, use, False, at_first(lambda: merged_turn(0)) if isinstance(n, int) else None)
            merge_down(t + 12, use + 2, n - 1, after=at_first(lambda: merged_turn(n)))

        g = MERGE_G // 2
        merge(MERGE_T, g, True)
        merge_slice(1)
        with pe.Fori(2, Q) as n:
            merge_slice(n)
        merge_down(FFN2_T - 4, g - 2 + 4 * Q, Q - 1, after=small_pieces, a=(mg_last_hi, mg_last_lo))

        def u_turn(i, half, use):
            pe.wait_ge(pair_read[half], use + 1)
            key = ("ffn2a", 0) if half == 0 else ("ffn2b", 0)
            for b in before[key]:
                bank_free(b, before[key][b] + i)
            turn(ubuf, (2 * half, 2 * half + 1)).then_inc(u_turned, 1)

        def ffn2_down(t, use, i, after=None, a=(h2_hi, h2_lo)):
            pe.wait_ge(h2_ready, i + 1)
            down(t, 0, use, *a, after)

        def ffn2(i):
            t = i * 12 + (FFN2_T - 4)
            use = i * 3 + (g - 2)
            project(t, 0, use, after=at_first(lambda: u_turn(0, 1, g)) if isinstance(i, int) else None)
            project(t + 4, 1, use, after=at_first(lambda: u_turn(i, 0, use)))
            ffn2_down(t + 8, use + 1, i - 1, after=at_first(lambda: u_turn(i, 1, use)))

        g = FFN2_G // 2
        project(FFN2_T, 0, g, 3, after=small_pieces)
        project(FFN2_T + 4, 1, g, after=at_first(lambda: u_turn(0, 0, g)))
        ffn2(1)
        with pe.Fori(2, NF) as i:
            ffn2(i)
        ffn2_down(TILES - 4, g - 2 + 3 * NF, NF - 1, a=(h2_last_hi, h2_last_lo))

    @block.scalar
    def _(act):
        def split(t, k):
            if isinstance(t, int) and t >= TILES:
                return
            act.wait_ge(raw_ready[k % RING], slot_count(t, k))
            if not (isinstance(t, int) and t < RING):
                act.wait_ge(tile_used, t - RING + 1)
            nc.scalar.activation(w_hi[:, k % RING], raw[:, k % RING], ACT.Copy).then_inc(hi_ready, 1)

        def copy(dst, src, scale=1.0, func=ACT.Copy, **kw):
            return nc.scalar.activation(dst, src, func, scale=scale, **kw)

        def read_group(t, pair, dst, scales, func=ACT.Copy):
            act.wait_ge(tile_used, t + 1)
            copy(dst[:, 0, :], acc[:, pair, 0, :], scales[:, 0:1], func)
            copy(dst[:, 1, :], acc[:, pair, 1, :], scales[:, 1:2], func).then_inc(pair_read[pair], 1)

        def xt_hi_piece(phase, q):
            act.wait_ge(xt_turned, 4 * phase + q + 1)
            gain = {0: gains[:, G_ATTN1:], 1: gains[:, G_FFN1:], 2: gain2[:, :], 3: gains[:, G_FFN2:]}[phase]
            banks = (0, 1) if q % 2 == 0 else (2, 3)
            for j in range(C):
                end = copy(xt_hi[:, C * q + j, :], misc[:, banks[j // 2], (j % 2) * S:(j % 2 + 1) * S],
                           gain[:, C * q + j:C * q + j + 1])
                if j % 2:
                    end.then_inc(xt_hi_done, 1)

        squares = [0]

        def square_sum(zn, tok, q):
            if squares[0]:
                act.wait_ge(sumsq_done, squares[0])
            nc.scalar.activation(junk[:, :], x[:, tok, q * N:(q + 1) * N], ACT.Square,
                                 accum_out=sumsq[:, zn, tok, q:q + 1]).then_inc(sumsq_done, 1)
            squares[0] += 1

        def root(zn):
            act.wait_ge(var_ready, zn + 1)
            nc.scalar.activation(sd[:, zn, :], var[:, zn, :], ACT.Sqrt).then_inc(sd_ready, 1)

        def attention(t):
            for r in range(8):
                s = t - WINDOW[r]
                probs, p_t, v = (probs1, pt1, v1) if r < 4 else (probs2, pt2, v2)
                head = HEAD0[r] - (4 if r > 5 else 0)
                head_am = head - (8 if r > 5 else 0)
                if KIND[r] == "R":
                    if 1 <= s < 3:
                        h = s - 1
                        act.wait_ge(values_done, HEAD0[r] + h + 1)
                        for qt in range(TOK):
                            src = misc[:, 2 + h, qt * RD:(qt + 1) * RD]
                            if ysquares[0] > 0:
                                act.wait_ge(ysq_done, ysquares[0])
                            nc.scalar.activation(junk[:, 0:RD], src, ACT.Square,
                                                 accum_out=hsum[:, 2 * h + qt:2 * h + qt + 1]).then_inc(ysq_done, 1)
                            ysquares[0] += 1
                        copy(ret_o[:, :, h * RD:(h + 1) * RD],
                             misc[:, 2 + h, :].rearrange("p (a b) -> p a b", a=TOK)).then_inc(drained[2 + h], 1)
                    if s == 3:
                        act.wait_ge(tile_used, t + 1)
                        n = ROUND_G[r] + 3
                        read_group(t, n % 2, ret_g, rstd[:, 3, :], ACT.Silu)
                        act.wait_ge(hvar_ready, r - 1)
                        nc.scalar.activation(hsd[:, 0:4], hvar[:, 0:4], ACT.Sqrt).then_inc(hsd_ready, 1)
                    if s == 5:
                        act.wait_ge(y_turned, r - 1)
                        for j in range(C):
                            c = 4 * (r - 4) + j
                            end = copy(ot_hi[:, c, :], misc[:, 2 + j // 2, (j % 2) * S:(j % 2 + 1) * S],
                                       gains[:, G_RET + c:G_RET + c + 1])
                            if j % 2:
                                end.then_inc(out_hi_done, 1)
                    continue
                if KIND[r] != "B" and 1 <= s < 5:
                    h = s - 1
                    act.wait_ge(rden_ready, head_am + h + 1)
                    for qt in range(TOK):
                        keys = keys_of(KIND[r], qt)
                        p = probs[:, h % 2, 0, qt, :] if r < 4 else probs[:, h % 2, qt, 0:keys]
                        end = copy(p, p, rden[:, h % 2, qt:qt + 1])
                    end.then_inc(probs_ready, 1)
                if 2 <= s < 6:
                    h = s - 2
                    act.wait_ge(probs_turned, head + h + 1)
                    if head + h > 0:
                        act.wait_ge(values_done, HEAD0[r] + h)
                    if KIND[r] == "M":
                        end = copy(pt2[:, :], misc[:, 2, 0:S + P])
                    else:
                        end = copy(p_t[:, :, :], misc[:, 2, :].rearrange("p (a b) -> p a b", a=TOK))
                    end.then_inc(drained[2], 1)
                if 0 <= s < 4:
                    h = s
                    n = head + h
                    act.wait_ge(npeak_ready, n + 1)
                    if KIND[r] == "B":
                        if h >= 2:
                            act.wait_ge(probs_turned, n - 1)
                        for c in range(2):
                            for qt in range(TOK):
                                k = 2 * c + qt
                                end = nc.scalar.activation(
                                    probs[:, h % 2, c, qt, :], misc[:, c, qt * S:(qt + 1) * S], ACT.Exp,
                                    bias=npeak[:, h % 2, k:k + 1], scale=64 ** -0.5,
                                    accum_out=den[:, h % 2, k:k + 1])
                            end.then_inc(drained[c], 1)
                    else:
                        for qt in range(TOK):
                            keys = keys_of(KIND[r], qt)
                            p = probs[:, h % 2, 0, qt, :] if r < 4 else probs[:, h % 2, qt, 0:keys]
                            kw = {"accum_out": den[:, h % 2, qt:qt + 1]} if KIND[r] == "M" else {}
                            end = nc.scalar.activation(p, p, ACT.Exp, bias=npeak[:, h % 2, qt:qt + 1], **kw)
                        end.then_inc(exp_done, 1)
                if 3 <= s < 7:
                    h = s - 3
                    act.wait_ge(values_done, HEAD0[r] + h + 1)
                    if KIND[r] == "B":
                        copy(ybuf[:, :, h * HD:(h + 1) * HD],
                             misc[:, 3, 0:S].rearrange("p (a b) -> p a b", a=TOK)).then_inc(drained[3], 1)
                    else:
                        if r < 4:
                            dst = yt_hi[:, r % Y_SLOTS, h, :]
                        else:
                            dst = mt_o_hi[:, 4 * (r - 6) + h, :]
                        copy(dst, misc[:, 3, 0:S]).then_inc(yhi_done, 1)
                if KIND[r] == "B" and s == 6:
                    act.wait_ge(drained[3], before[("values", r, 3)][3] + 1)
                    act.wait_ge(probs_turned, head + 4)
                    nc.scalar.activation(probs1[:, 0].rearrange("p c a b -> p (c a b)"),
                                         ybuf[:, :, :].rearrange("p a b -> p (a b)"),
                                         ACT.Square).then_inc(ysq_done, 1)
                    ysquares[0] += 1
                    act.wait_ge(hvar_ready, r - 1)
                    nc.scalar.activation(hsd[:, :], hvar[:, :], ACT.Sqrt).then_inc(hsd_ready, 1)
                if KIND[r] == "B" and s == 8:
                    act.wait_ge(y_turned, r - 1)
                    for b in range(2):
                        copy(yt_hi[:, r % Y_SLOTS, 2 * b:2 * b + 2, :],
                             misc[:, 2 + b, :].rearrange("p (a b) -> p a b", a=2), sub8[:, 0:1]).then_inc(out_hi_done, 1)

        ysquares = [0]

        def projections(t):
            for r in range(8):
                rs = rstd[:, 0, :] if r < 4 else rstd[:, 3, :]
                for j in range(2):
                    if t == ROUND_T[r] + 4 * j + 3:
                        n = ROUND_G[r] + j
                        if 2 * r + j > 0:
                            act.wait_ge(stage_turned, 2 * r + j)
                        act.wait_ge(tile_used, t + 1)
                        st = stage1 if r < 4 else stage2
                        copy(st[:, 0, :], acc[:, n % 2, 0, :], rs[:, 0:1])
                        copy(st[:, 1, :], acc[:, n % 2, 1, :], rs[:, 1:2]).then_inc(pair_read[n % 2], 1)
                    if t == ROUND_T[r] + TURN[j]:
                        act.wait_ge(stage_turned, 2 * r + j + 1)
                        dst = (qt1, kt1)[j] if r < 4 else (qt2, kt2)[j]
                        copy(dst[:, 0:2, :], misc[:, 0, :].rearrange("p (a b) -> p a b", a=2)).then_inc(drained[0], 1)
                if t == ROUND_T[r] + 11:
                    n = ROUND_G[r] + 2
                    act.wait_ge(tile_used, t + 1)
                    vv = v1 if r < 4 else v2
                    copy(vv[:, 0, :], acc[:, n % 2, 0, :], rs[:, 0:1])
                    copy(vv[:, 1, :], acc[:, n % 2, 1, :], rs[:, 1:2]).then_inc(pair_read[n % 2], 1)

        def start(t):
            if t in (0, 1):
                for q in (2 * t, 2 * t + 1):
                    act.wait_ge(x_loaded[q], 16)
                    for tok in range(TOK):
                        square_sum(0, tok, q)
            if t == 2:
                root(0)
                act.wait_ge(lam_sums_ready, 1)
                nc.scalar.activation(lams[:, 2:4], lams[:, 0:2], ACT.Exp).then_inc(lam_exp_done, 1)
                act.wait_ge(rstd_ready, 1)
                act.wait_ge(sub8_done, 1)

        def pieces(t):
            start(t)
            attention(t)
            projections(t)
            for phase, t_last in ((1, DOWN_T[3]), (3, FFN2_T - 4)):
                if 1 <= t - t_last < 5:
                    xt_hi_piece(phase, t - t_last - 1)
                if 0 <= t - t_last < 4:
                    zn = {1: 1, 3: 4}[phase]
                    x_quarter(act, zn, t - t_last)
                    for tok in range(TOK):
                        square_sum(zn, tok, t - t_last)

        act.wait_ge(gains_loaded, 16)
        copy(sub8[:, :], gains[:, G_SUBLN:G_SUBLN + 1], 1.0 - LAM_INIT).then_inc(sub8_done, 1)
        for t in range(LEAD):
            if t < 2:
                xt_hi_piece(0, t)
            split(t, t)

        for t in range(FFN1_T):
            if t in (0, 1):
                xt_hi_piece(0, t + 2)
            split(t + LEAD, t + LEAD)
            pieces(t)

        def read_gate(t):
            act.wait_ge(tile_used, t + 1)
            copy(gate[:, 0, :], acc[:, 0, 0, :], rstd[:, 1, 0:1], ACT.Silu)
            copy(gate[:, 1, :], acc[:, 0, 1, :], rstd[:, 1, 1:2], ACT.Silu).then_inc(pair_read[0], 1)

        def hid_hi(i, dst=ht_hi):
            act.wait_ge(hid_turned, i + 1)
            for b in range(2):
                copy(dst[:, 2 * b:2 * b + 2, :],
                     misc[:, b, :].rearrange("p (a b) -> p a b", a=2)).then_inc(hid_hi_done, 1)

        for k in range(8):
            split(FFN1_T + k + LEAD, k + LEAD)
            if k == 0:
                pieces(FFN1_T)
            if k == 1:
                root(1)
            if k == 3:
                act.wait_ge(rstd_ready, 2)
                read_gate(FFN1_T + k)
        hid_hi(0)

        def ffn1(i):
            last = isinstance(i, int)
            t = i * 12 + (FFN1_T - 4)
            for k in range(12):
                split(t + k + LEAD, k + LEAD)
                if k == 3:
                    act.wait_ge(pair_read[1], i * 3 + (FFN1_G // 2 - 3))
                    read_gate(t + k)
                if k == 9 and last:
                    hid_hi(i, ht_last_hi)
                if k == 11 and not last:
                    act.wait_ge(tile_used, t + k + 1)
                    hid_hi(i)

        with act.Fori(1, NF - 1) as i:
            ffn1(i)
        ffn1(NF - 1)
        for k in range(4):
            t = ROUND_T[4] - 4 + k
            split(t + LEAD, k + LEAD)
            x_quarter(act, 2, k)
            for tok in range(TOK):
                square_sum(2, tok, k)
            if k > 0:
                xt_hi_piece(2, k - 1)

        for t in range(ROUND_T[4], MERGE_T):
            split(t + LEAD, t + LEAD)
            if t == ROUND_T[4]:
                xt_hi_piece(2, 3)
                root(2)
            if t in (ROUND_T[4] + 1, ROUND_T[4] + 2):
                for q in range(2 * (t - ROUND_T[4]) - 2, 2 * (t - ROUND_T[4])):
                    act.wait_ge(x_gained, q + 1)
                    for tok in range(TOK):
                        square_sum(3, tok, q)
            if t == ROUND_T[4] + 2:
                root(3)
            if t == ROUND_T[4] + 3:
                act.wait_ge(rstd_ready, 4)
            pieces(t)

        def sigmoid(t, pair, dst):
            act.wait_ge(tile_used, t + 1)
            copy(dst[:, 0, :], acc[:, pair, 0, :], rstd[:, 3, 0:1], ACT.Sigmoid)
            copy(dst[:, 1, :], acc[:, pair, 1, :], rstd[:, 3, 1:2], ACT.Sigmoid).then_inc(pair_read[pair], 1)

        def merged_hi(n, dst=mg_hi):
            act.wait_ge(merged_turned, n + 1)
            for b in range(2):
                copy(dst[:, 2 * b:2 * b + 2, :],
                     misc[:, b, :].rearrange("p (a b) -> p a b", a=2)).then_inc(merged_hi_done, 1)

        for k in range(12):
            t = MERGE_T + k
            split(t + LEAD, k + LEAD)
            if k == 7:
                act.wait_ge(scores_done, HEAD0[7] + 4)
            if k in (3, 7):
                sigmoid(t, k // 4, (sig_ret, sig_moba)[k // 4])
            pieces(t)
        act.wait_ge(values_done, HEAD0[7] + 4)
        merged_hi(0)

        def merge(n):
            last = isinstance(n, int)
            t = n * 16 + (MERGE_T - 4)
            for k in range(16):
                split(t + k + LEAD, k + LEAD)
                if k == 3:
                    act.wait_ge(merged_ready, n)
                    sigmoid(t + k, 0, sig_ret)
                if k == 7:
                    act.wait_ge(merged_turned, n)
                    sigmoid(t + k, 1, sig_moba)
                if k == 13 and last:
                    merged_hi(n, mg_last_hi)
                if k == 15 and not last:
                    act.wait_ge(tile_used, t + k + 1)
                    merged_hi(n)

        with act.Fori(1, Q - 1) as n:
            merge(n)
        merge(Q - 1)
        for k in range(4):
            t = FFN2_T - 4 + k
            split(t + LEAD, k + LEAD)
            pieces(t)

        def u_copy(i, half, t):
            act.wait_ge(u_turned, i * 2 + half)
            act.wait_ge(tile_used, t + 1)
            copy(ubuf[:, 0, :], acc[:, half, 0, :], rstd[:, 4, 0:1])
            copy(ubuf[:, 1, :], acc[:, half, 1, :], rstd[:, 4, 1:2]).then_inc(pair_read[half], 1)

        def last_tap(i, half, dst):
            act.wait_ge(u_turned, i * 2 + half + 1)
            for j in range(C):
                col = i * C + (half * FF // P + j)
                src = misc[:, 2 * half + j // 2, (j % 2) * S:(j % 2 + 1) * S]
                end = nc.scalar.activation(dst[:, j, :], src, ACT.Identity, bias=taps[:, 3, bass.ds(col, 1)],
                                           scale=taps[:, 2, bass.ds(col, 1)])
                if j % 2:
                    end.then_inc(tap2_done, 1)

        def silu_a(i):
            act.wait_ge(drained[1], i + (before[("ffn2a", 0)][1] + 1))
            nc.scalar.activation(conv_a[:], conv_a[:], ACT.Silu).then_inc(silu_done, 1)

        def product_hi(i, dst=h2_hi):
            act.wait_ge(prod_done, i + 1)
            copy(dst[:], conv_a[:]).then_inc(h2_hi_done, 1)

        for k in range(8):
            t = FFN2_T + k
            split(t + LEAD, k + LEAD)
            if k == 0:
                pieces(t)
            if k == 1:
                root(4)
            if k == 3:
                act.wait_ge(rstd_ready, 5)
                act.wait_ge(tile_used, t + 1)
                copy(ubuf[:, 0, :], acc[:, 0, 0, :], rstd[:, 4, 0:1])
                copy(ubuf[:, 1, :], acc[:, 0, 1, :], rstd[:, 4, 1:2]).then_inc(pair_read[0], 1)
            if k == 5:
                last_tap(0, 0, conv_a)
            if k == 6:
                silu_a(0)
            if k == 7:
                u_copy(0, 1, t)

        def ffn2(i):
            first, last = (isinstance(i, int) and i == j for j in (1, NF - 1))
            t = i * 12 + (FFN2_T - 4)
            for k in range(12):
                split(t + k + LEAD, k + LEAD)
                if k == 0 and first:
                    last_tap(0, 1, conv_b)
                if k == 1 and first:
                    product_hi(0)
                if k == 3:
                    u_copy(i, 0, t + k)
                if k == 5:
                    act.wait_ge(h2_ready, i)
                    last_tap(i, 0, conv_a)
                if k == 6:
                    silu_a(i)
                if k == 7:
                    u_copy(i, 1, t + k)
                if k == 8:
                    last_tap(i, 1, conv_b)
                if k == 10 and last:
                    product_hi(i, h2_last_hi)
                if k == 11 and not last:
                    act.wait_ge(tile_used, t + k + 1)
                    product_hi(i)

        ffn2(1)
        with act.Fori(2, NF - 1) as i:
            ffn2(i)
        ffn2(NF - 1)
        for k in range(4):
            t = TILES - 4 + k
            split(t + LEAD, k + LEAD)
            if k == 3:
                nc.scalar.activation(sd[:, 5, :], var[:, 4, :], ACT.Sqrt).then_inc(table_loaded, 1)
            x_quarter(act, 5, k)
            for tok in range(TOK):
                square_sum(5, tok, k)
        act.wait_ge(table_loaded, 1)
        root(5)
        act.wait_ge(rstd_ready, 6)
        act.wait_ge(x_gained, Q + 3)
        for cols in (slice(0, D // 2), slice(D // 2, 3 * N)):
            copy(x[:, 1, cols], x[:, 1, cols], rstd[:, 5, 1:2]).then_inc(out_act_ready, 1)

    @block.vector
    def _(dve):
        links = [0]

        def link(ins_):
            ins_.then_inc(dve_link, 1)
            links[0] += 1
            dve.wait_ge(dve_link, links[0])

        def split(t, k):
            if isinstance(t, int) and t >= TILES:
                return
            dve.wait_ge(raw_ready[k % RING], slot_count(t, k))
            dve.wait_ge(hi_ready, t + 1)
            nc.vector.tensor_tensor(w_lo[:, k % RING], raw[:, k % RING], w_hi[:, k % RING].bitcast(F32),
                                    ALU.subtract).then_inc(lo_ready, 1)

        def minus_hi(dst, src, hi, gain=None):
            if gain is None:
                return nc.vector.tensor_tensor(dst, src, hi.bitcast(F32), ALU.subtract)
            return nc.vector.scalar_tensor_tensor(out=dst, in0=src, scalar=gain, in1=hi.bitcast(F32),
                                                  op0=ALU.mult, op1=ALU.subtract)

        def xt_lo_piece(phase, q):
            gain = {0: gains[:, G_ATTN1:], 1: gains[:, G_FFN1:], 2: gain2[:, :], 3: gains[:, G_FFN2:]}[phase]
            banks = (0, 1) if q % 2 == 0 else (2, 3)
            for j in range(C):
                if j % 2 == 0:
                    dve.wait_ge(xt_hi_done, 2 * (4 * phase + q) + j // 2 + 1)
                c = C * q + j
                end = minus_hi(xt_lo[:, c, :], misc[:, banks[j // 2], (j % 2) * S:(j % 2 + 1) * S],
                               xt_hi[:, c, :], gain[:, c:c + 1])
                if j % 2:
                    end.then_inc(drained[banks[j // 2]], 1)

        def add_group(t, pair, n):
            dve.wait_ge(tile_used, t + 1)
            for tok in range(TOK):
                xs = x[:, tok, n * N:(n + 1) * N]
                end = nc.vector.tensor_tensor(xs, acc[:, pair, tok, :], xs, ALU.add)
            end.then_inc(pair_read[pair], 1)

        def gain_quarter(q):
            for tok in range(TOK):
                xs = x[:, tok, q * N:(q + 1) * N]
                end = nc.vector.tensor_tensor(xs, xs, final_row[:, q * N:(q + 1) * N], ALU.mult)
            end.then_inc(x_gained, 1)

        def variance(zn):
            dve.wait_ge(sumsq_done, 8 * (zn + 1))
            link(nc.vector.tensor_reduce(var[:, zn, :], sumsq[:, zn], AX_X, ALU.add))
            if zn == 3:
                for tok in range(TOK):
                    end = nc.vector.tensor_scalar(var[:, zn, tok:tok + 1], var[:, zn, tok:tok + 1],
                                                  rstd[:, 2, tok:tok + 1], rstd[:, 2, tok:tok + 1], ALU.mult, ALU.mult)
                link(end)
            nc.vector.tensor_scalar(var[:, zn, :], var[:, zn, :], 1.0 / D, 1e-6, ALU.mult,
                                    ALU.add).then_inc(var_ready, 1)

        def inverse(zn):
            dve.wait_ge(sd_ready, zn + 1)
            if zn != 3:
                nc.vector.reciprocal(rstd[:, zn, :], sd[:, zn, :]).then_inc(rstd_ready, 1)
            else:
                link(nc.vector.reciprocal(rstd[:, zn, :], sd[:, zn, :]))
                nc.vector.tensor_tensor(rstd[:, zn, :], rstd[:, zn, :], rstd[:, 2, :],
                                        ALU.mult).then_inc(rstd_ready, 1)

        def rope(r, j):
            n = 2 * r + j
            g = ROUND_G[r] + j
            st = stage1 if r < 4 else stage2
            dve.wait_ge(pair_read[g % 2], g // 2 + 1)
            nh, tab = {"A": (4, rope_a), "B": (8, rope_b), "R": (2, rope_r), "M": (4, rope_a)}[KIND[r]]
            rot = tab.shape[-1]
            half = rot // 2
            xs = st[:, :, :].rearrange("p a (h d) -> p a h d", h=nh)
            if KIND[r] == "R":
                tmp = ret_o[:, :, :].rearrange("p a (h d) -> p a h d", h=nh)
            else:
                tmp = junk[:, 0:TOK * nh * rot].rearrange("p (a h d) -> p a h d", a=TOK, h=nh)

            def table(k, lo, hi):
                w = hi - lo
                return tab[:, k, :, lo:hi].unsqueeze(2).to_broadcast([P, TOK, nh, w])

            nc.vector.tensor_tensor(tmp[:, :, :, 0:half], xs[:, :, :, half:rot], table(1, 0, half), ALU.mult)
            link(nc.vector.tensor_tensor(tmp[:, :, :, half:rot], xs[:, :, :, 0:half], table(1, half, rot), ALU.mult))
            link(nc.vector.tensor_tensor(xs[:, :, :, 0:rot], xs[:, :, :, 0:rot], table(0, 0, rot), ALU.mult))
            nc.vector.tensor_tensor(xs[:, :, :, 0:rot], xs[:, :, :, 0:rot], tmp[:, :, :, :],
                                    ALU.add).then_inc(stage_roped, 1)

        def attention(t):
            for r in range(8):
                s = t - WINDOW[r]
                probs = probs1 if r < 4 else probs2
                head = HEAD0[r] - (4 if r > 5 else 0)
                if KIND[r] == "R":
                    if 0 <= s < 2:
                        h = s
                        dve.wait_ge(scores_done, HEAD0[r] + h + 1)
                        if r > 4:
                            dve.wait_ge(values_done, HEAD0[r - 1] + h + 1)
                        nc.vector.tensor_tensor(ret_s[:, h, 0:S], misc[:, h, 0:S],
                                                decay[:, 2 * part(r) + h, 0:S], ALU.mult)
                        nc.vector.tensor_tensor(ret_s[:, h, S:], misc[:, h, S:S + P],
                                                decay[:, 2 * part(r) + h, S:], ALU.mult).then_inc(drained[h], 1)
                    if s == 2:
                        dve.wait_ge(ysq_done, 2 + 4 * (r - 3))
                        nc.vector.tensor_scalar(hvar[:, 0:4], hsum[:, 0:4], 1.0 / RD, 1e-6, ALU.mult,
                                                ALU.add).then_inc(hvar_ready, 1)
                    if s == 4:
                        dve.wait_ge(hsd_ready, r - 1)
                        link(nc.vector.reciprocal(hrs[:, 0:4], hsd[:, 0:4]))
                        n = ROUND_G[r] + 3
                        dve.wait_ge(pair_read[n % 2], n // 2 + 1)
                        for h in range(2):
                            for qt in range(TOK):
                                o = ret_o[:, qt, h * RD:(h + 1) * RD]
                                end = nc.vector.scalar_tensor_tensor(
                                    out=o, in0=o, scalar=hrs[:, 2 * h + qt:2 * h + qt + 1],
                                    in1=ret_g[:, qt, h * RD:(h + 1) * RD], op0=ALU.mult, op1=ALU.mult)
                        end.then_inc(y_normed, 1)
                    if s == 5:
                        for j in range(C):
                            c = 4 * (r - 4) + j
                            if j % 2 == 0:
                                dve.wait_ge(out_hi_done, 2 * (r - 2) + j // 2 + 1)
                            end = minus_hi(ot_lo[:, c, :], misc[:, 2 + j // 2, (j % 2) * S:(j % 2 + 1) * S],
                                           ot_hi[:, c, :], gains[:, G_RET + c:G_RET + c + 1])
                            if j % 2:
                                end.then_inc(drained[2 + j // 2], 1)
                    continue
                def sums():
                    h = s - 1
                    if KIND[r] == "B":
                        dve.wait_ge(drained[1], before[("scores", r, h)][1] + 1)
                    else:
                        dve.wait_ge(exp_done, head - (8 if r > 5 else 0) + h + 1)
                    if KIND[r] == "A":
                        for qt in range(TOK):
                            p = probs[:, h % 2, 0, qt, :]
                            end = nc.vector.tensor_tensor_reduce(p, p, mult_a[:, qt, :], 1.0, 0.0, ALU.mult,
                                                                 ALU.add, den[:, h % 2, qt:qt + 1])
                        link(end)
                        nc.vector.reciprocal(rden[:, h % 2, 0:2], den[:, h % 2, 0:2]).then_inc(rden_ready, 1)
                    elif KIND[r] == "M":
                        nc.vector.reciprocal(rden[:, h % 2, 0:2], den[:, h % 2, 0:2]).then_inc(rden_ready, 1)
                    else:
                        link(nc.vector.reciprocal(rden[:, h % 2, :], den[:, h % 2, :]))
                        link(nc.vector.tensor_scalar(rden[:, h % 2, 2:4], rden[:, h % 2, 2:4], nlam[:, 0:1], None,
                                                     ALU.mult))
                        for qt in range(TOK):
                            p1 = probs[:, h % 2, 1, qt, :]
                            end = nc.vector.tensor_scalar(p1, p1, rden[:, h % 2, 2 + qt:3 + qt], None, ALU.mult)
                        link(end)
                        for qt in range(TOK):
                            p0 = probs[:, h % 2, 0, qt, :]
                            end = nc.vector.scalar_tensor_tensor(
                                out=p0, in0=p0, scalar=rden[:, h % 2, qt:qt + 1], in1=probs[:, h % 2, 1, qt, :],
                                op0=ALU.mult, op1=ALU.add)
                        end.then_inc(probs_ready, 1)

                def maximum():
                    h = s
                    n = head + h
                    dve.wait_ge(scores_done, HEAD0[r] + h + 1)
                    if KIND[r] == "B":
                        for c in range(2):
                            end = nc.vector.tensor_reduce(peak[:, h % 2, 2 * c:2 * c + 2],
                                                          misc[:, c, :].rearrange("p (a b) -> p a b", a=TOK),
                                                          AX_X, ALU.max)
                        link(end)
                        nc.vector.tensor_scalar(npeak[:, h % 2, :], peak[:, h % 2, :], -(64 ** -0.5), None,
                                                ALU.mult).then_inc(npeak_ready, 1)
                    else:
                        if n >= 2:
                            dve.wait_ge(probs_turned, n - 1)
                        p = probs[:, h % 2, 0] if r < 4 else probs[:, h % 2]
                        mask = mask_a if KIND[r] == "A" else causal
                        for qt in range(TOK):
                            keys = keys_of(KIND[r], qt)
                            end = nc.vector.scalar_tensor_tensor(
                                out=p[:, qt, 0:keys], in0=misc[:, 0, qt * S:qt * S + keys], scalar=HD ** -0.5,
                                in1=mask[:, qt, 0:keys], op0=ALU.mult, op1=ALU.add)
                        end.then_inc(drained[0], 1)
                        dve.wait_ge(drained[0], before[("scores", r, h)][0] + 1)
                        for qt in range(TOK):
                            end = nc.vector.tensor_reduce(peak[:, h % 2, qt:qt + 1],
                                                          p[:, qt, 0:keys_of(KIND[r], qt)], AX_X, ALU.max)
                        link(end)
                        nc.vector.tensor_scalar(npeak[:, h % 2, 0:2], peak[:, h % 2, 0:2], -1.0, None,
                                                ALU.mult).then_inc(npeak_ready, 1)

                if KIND[r] == "B" and 0 <= s < 4:
                    maximum()
                if 1 <= s < 5:
                    sums()
                if KIND[r] != "B" and 0 <= s < 4:
                    maximum()
                if KIND[r] != "B" and 3 <= s < 7:
                    h = s - 3
                    dve.wait_ge(yhi_done, HEAD0[r] + h + 1 - (12 if r > 5 else 0))
                    if r < 4:
                        slot = r % Y_SLOTS
                        end = minus_hi(yt_lo[:, slot, h, :], misc[:, 3, 0:S], yt_hi[:, slot, h, :])
                    else:
                        c = 4 * (r - 6) + h
                        end = minus_hi(mt_o_lo[:, c, :], misc[:, 3, 0:S], mt_o_hi[:, c, :])
                    end.then_inc(drained[3], 1)
                if KIND[r] == "B" and s == 6:
                    dve.wait_ge(ysq_done, r - 1)
                    link(nc.vector.tensor_reduce(
                        hvar[:, :], probs1[:, 0].rearrange("p c a b -> p (c a b)").rearrange("p (h d) -> p h d", d=HD),
                        AX_X, ALU.add))
                    nc.vector.tensor_scalar(hvar[:, :], hvar[:, :], 1.0 / HD, 1e-5, ALU.mult,
                                            ALU.add).then_inc(hvar_ready, 1)
                    dve.wait_ge(hsd_ready, r - 1)
                    link(nc.vector.reciprocal(hrs[:, :], hsd[:, :]))
                    yv = ybuf[:, :, :].rearrange("p a (h d) -> p (a h) d", d=HD)
                    nc.vector.tensor_tensor(yv, yv, hrs[:, :].unsqueeze(2).to_broadcast([P, 8, HD]),
                                            ALU.mult).then_inc(y_normed, 1)
                if KIND[r] == "B" and s == 8:
                    slot = r % Y_SLOTS
                    for b in range(2):
                        dve.wait_ge(out_hi_done, 2 * (r - 2) + b + 1)
                        minus_hi(yt_lo[:, slot, 2 * b:2 * b + 2, :],
                                 misc[:, 2 + b, :].rearrange("p (a b) -> p a b", a=2),
                                 yt_hi[:, slot, 2 * b:2 * b + 2, :], sub8[:, 0:1]).then_inc(drained[2 + b], 1)

        def projections(t):
            for r in range(8):
                for j in range(2):
                    if t == ROUND_T[r] + 4 * j + 3:
                        rope(r, j)
                    if t == ROUND_T[r] + TURN[j]:
                        dve.wait_ge(stage_turned, 2 * r + j + 1)
                        dst = (qt1, kt1)[j] if r < 4 else (qt2, kt2)[j]
                        nc.vector.tensor_copy(dst[:, 2:4, :],
                                              misc[:, 1, :].rearrange("p (a b) -> p a b", a=2)).then_inc(drained[1], 1)

        def residual(t):
            for i in range(4):
                n = t - DOWN_T[i]
                if 0 <= n < 4:
                    g = DOWN_G[i] + n
                    add_group(t, g % 2, n)
            n = t - (FFN2_T - 4)
            if 0 <= n < 4:
                add_group(t, n % 2, n)

        def start(t):
            if t == 2:
                variance(0)
                dve.wait_ge(lam_loaded, 16)
                link(nc.vector.tensor_tensor(lq[:, 0:4:2, :], lq[:, 0:4:2, :], lq[:, 1:4:2, :], ALU.mult))
                nc.vector.tensor_reduce(lams[:, 0:2], lq[:, 0:4:2, :], AX_X, ALU.add).then_inc(lam_sums_ready, 1)
                inverse(0)
                dve.wait_ge(lam_exp_done, 1)
                link(nc.vector.tensor_tensor(nlam[:, :], lams[:, 3:4], lams[:, 2:3], ALU.subtract))
                link(nc.vector.tensor_scalar(nlam[:, :], nlam[:, :], -LAM_INIT, None, ALU.add))
                dve.wait_ge(ropes_loaded, 16 * 2)
                dve.wait_ge(sub8_done, 1)
            if t == WINDOW[0]:
                dve.wait_ge(tables_loaded, 16 * 3)

        def pieces(t):
            start(t)
            attention(t)
            projections(t)
            residual(t)
            for phase, t_last in ((1, DOWN_T[3]), (3, FFN2_T - 4)):
                if 1 <= t - t_last < 5:
                    xt_lo_piece(phase, t - t_last - 1)

        def softmax_step(t):
            return any(KIND[r] != "R" and 0 <= t - WINDOW[r] < 9 for r in range(8))

        dve.wait_ge(gains_loaded, 16)
        for t in range(LEAD):
            if t < 2:
                xt_lo_piece(0, t)
            split(t, t)
        link(nc.vector.tensor_tensor(gain2[:, :], gains[:, G_FINAL:G_FINAL + KD], gains[:, G_ATTN2:G_ATTN2 + KD],
                                     ALU.mult))
        for t in range(FFN1_T):
            if t in (0, 1):
                xt_lo_piece(0, t + 2)
            if softmax_step(t):
                pieces(t)
            split(t + LEAD, t + LEAD)
            if not softmax_step(t):
                pieces(t)

        def gated(i, t, use):
            dve.wait_ge(pair_read[0], use + 1)
            if not (isinstance(i, int) and i == 0):
                dve.wait_ge(hid_turned, i)
            dve.wait_ge(tile_used, t + 1)
            for tok in range(TOK):
                end = nc.vector.scalar_tensor_tensor(out=hid[:, tok, :], in0=acc[:, 1, tok, :],
                                                     scalar=rstd[:, 1, tok:tok + 1], in1=gate[:, tok, :],
                                                     op0=ALU.mult, op1=ALU.mult)
            end.then_inc(pair_read[1], 1)

        def hid_lo(i, hi=ht_hi, lo=ht_lo):
            for b in range(2):
                dve.wait_ge(hid_hi_done, i * 2 + b + 1)
                minus_hi(lo[:, 2 * b:2 * b + 2, :], misc[:, b, :].rearrange("p (a b) -> p a b", a=2),
                         hi[:, 2 * b:2 * b + 2, :]).then_inc(drained[b], 1)

        for k in range(8):
            t = FFN1_T + k
            split(t + LEAD, k + LEAD)
            if k == 0:
                pieces(t)
            if k == 1:
                variance(1)
                inverse(1)
            if k == 7:
                gated(0, t, FFN1_G // 2)
        hid_lo(0)

        def ffn1(i):
            last = isinstance(i, int)
            t = i * 12 + (FFN1_T - 4)
            for k in range(12):
                split(t + k + LEAD, k + LEAD)
                if k == 7:
                    gated(i, t + k, i * 3 + (FFN1_G // 2 - 2))
                if k >= 8:
                    add_group(t + k, k % 2, k - 8)
                if k == 9 and last:
                    hid_lo(i, ht_last_hi, ht_last_lo)
                if k == 11 and not last:
                    hid_lo(i)

        with dve.Fori(1, NF - 1) as i:
            ffn1(i)
        ffn1(NF - 1)
        for k in range(4):
            t = ROUND_T[4] - 4 + k
            split(t + LEAD, k + LEAD)
            add_group(t, k % 2, k)
            if k > 0:
                xt_lo_piece(2, k - 1)

        for t in range(ROUND_T[4], MERGE_T):
            if softmax_step(t):
                pieces(t)
            split(t + LEAD, t + LEAD)
            if t == ROUND_T[4]:
                dve.wait_ge(sumsq_done, 8 * 3)
                dve.wait_ge(row_loaded, 16)
                for q in range(3):
                    gain_quarter(q)
                xt_lo_piece(2, 3)
                variance(2)
                inverse(2)
                gain_quarter(3)
            if t == ROUND_T[4] + 2:
                variance(3)
                inverse(3)
                dve.wait_ge(tables2_loaded, 16 * 3)
            for tok in range(TOK):
                if t == ROUND_T[4] + 3 + 2 * tok:
                    nc.vector.tensor_scalar(x[:, tok, :], x[:, tok, :], rstd[:, 2, tok:tok + 1], None, ALU.mult)
            if not softmax_step(t):
                pieces(t)

        def merge_pieces(n, t, k, use):
            if k == 9:
                dve.wait_ge(pair_read[0], use + 1)
                dve.wait_ge(tile_used, t + 1)
                for tok in range(TOK):
                    end = nc.vector.tensor_tensor(sig_ret[:, tok, :], acc[:, 0, tok, :], sig_ret[:, tok, :], ALU.mult)
                end.then_inc(pair_read[0], 1)
            if k == 11:
                dve.wait_ge(pair_read[1], use + 1)
                dve.wait_ge(tile_used, t + 1)
                for tok in range(TOK):
                    end = nc.vector.tensor_tensor(sig_moba[:, tok, :], acc[:, 1, tok, :], sig_moba[:, tok, :],
                                                  ALU.mult)
                end.then_inc(pair_read[1], 1)
                dve.wait_ge(pair_read[1], use + 2)
                nc.vector.tensor_tensor(sig_moba[:], sig_moba[:], sig_ret[:], ALU.add).then_inc(merged_ready, 1)

        def merged_lo(n, hi=mg_hi, lo=mg_lo):
            for b in range(2):
                dve.wait_ge(merged_hi_done, n * 2 + b + 1)
                minus_hi(lo[:, 2 * b:2 * b + 2, :], misc[:, b, :].rearrange("p (a b) -> p a b", a=2),
                         hi[:, 2 * b:2 * b + 2, :]).then_inc(drained[b], 1)

        for k in range(12):
            t = MERGE_T + k
            if softmax_step(t):
                pieces(t)
            split(t + LEAD, k + LEAD)
            merge_pieces(0, t, k, MERGE_G // 2)
            if not softmax_step(t):
                pieces(t)
        merged_lo(0)

        def merge(n):
            last = isinstance(n, int)
            t = n * 16 + (MERGE_T - 4)
            for k in range(16):
                split(t + k + LEAD, k + LEAD)
                merge_pieces(n, t + k, k, n * 4 + (MERGE_G // 2 - 2))
                if k >= 12:
                    add_group(t + k, k % 2, k - 12)
                if k == 13 and last:
                    merged_lo(n, mg_last_hi, mg_last_lo)
                if k == 15 and not last:
                    merged_lo(n)

        with dve.Fori(1, Q - 1) as n:
            merge(n)
        merge(Q - 1)
        for k in range(4):
            t = FFN2_T - 4 + k
            split(t + LEAD, k + LEAD)
            pieces(t)

        def taps_on(i, half, dst):
            for w, gone in ((1, 1), (0, 2)):
                for j in range(C):
                    if j % 2 == 0:
                        if w == 1:
                            dve.wait_ge(tap2_done, i * 4 + (2 * half + j // 2 + 1))
                        else:
                            dve.wait_ge(tap1_done, i * 4 + (2 * half + j // 2 + 1))
                    col = i * C + (half * FF // P + j)
                    src = misc[:, 2 * half + j // 2, (j % 2) * S:(j % 2 + 1) * S - gone]
                    end = nc.vector.scalar_tensor_tensor(out=dst[:, j, gone:], in0=src,
                                                         scalar=taps[:, w, bass.ds(col, 1)], in1=dst[:, j, gone:],
                                                         op0=ALU.mult, op1=ALU.add)
                    if w == 1 and j % 2:
                        end.then_inc(tap1_done, 1)
                    if w == 0 and j % 2:
                        end.then_inc(drained[2 * half + j // 2], 1)

        def product(i):
            dve.wait_ge(silu_done, i + 1)
            dve.wait_ge(drained[3], i + (before[("ffn2b", 0)][3] + 1))
            nc.vector.tensor_tensor(conv_a[:], conv_a[:], conv_b[:], ALU.mult).then_inc(prod_done, 1)

        def product_lo(i, hi=h2_hi, lo=h2_lo):
            dve.wait_ge(h2_hi_done, i + 1)
            nc.vector.tensor_tensor(lo[:], conv_a[:], hi[:].bitcast(F32), ALU.subtract).then_inc(h2_ready, 1)

        for k in range(8):
            t = FFN2_T + k
            split(t + LEAD, k + LEAD)
            if k == 0:
                pieces(t)
            if k == 1:
                variance(4)
                inverse(4)
            if k == 5:
                taps_on(0, 0, conv_a)

        def ffn2(i):
            first, last = (isinstance(i, int) and i == j for j in (1, NF - 1))
            t = i * 12 + (FFN2_T - 4)
            for k in range(12):
                split(t + k + LEAD, k + LEAD)
                if k == 0 and first:
                    taps_on(0, 1, conv_b)
                if k == 1 and first:
                    product(0)
                    product_lo(0)
                if k == 5:
                    taps_on(i, 0, conv_a)
                if k == 9:
                    taps_on(i, 1, conv_b)
                if k == (9 if last else 10):
                    product(i)
                if k >= 8:
                    add_group(t + k, k % 2, k - 8)
                if k == 10 and last:
                    product_lo(i, h2_last_hi, h2_last_lo)
                if k == 11 and not last:
                    product_lo(i)

        ffn2(1)
        with dve.Fori(2, NF - 1) as i:
            ffn2(i)
        ffn2(NF - 1)
        for k in range(4):
            t = TILES - 4 + k
            split(t + LEAD, k + LEAD)
            if k == 0:
                dve.wait_ge(row_loaded, 32)
            else:
                dve.wait_ge(sumsq_done, 40 + 2 * k)
                gain_quarter(k - 1)
            add_group(t, k % 2, k)
        variance(5)
        inverse(5)
        dve.wait_ge(rstd_ready, 6)
        for cols in (slice(0, D // 2), slice(D // 2, 3 * N)):
            end = nc.vector.tensor_scalar(x[:, 0, cols], x[:, 0, cols], rstd[:, 5, 0:1], None, ALU.mult)
            if cols.start == 0:
                end.then_inc(out_dve_ready, 1)
        for tok in range(TOK):
            xs = x[:, tok, 3 * N:]
            nc.vector.scalar_tensor_tensor(out=xs, in0=xs, scalar=rstd[:, 5, tok:tok + 1], in1=final_row[:, 3 * N:],
                                           op0=ALU.mult, op1=ALU.mult).then_inc(out_dve_ready, 1)

    ctx.close()


def tables():
    f32 = np.float32
    i = np.arange(S)
    by_tile = lambda a: np.ascontiguousarray(a.reshape(TOK, P, -1).transpose(1, 0, 2))
    times = np.zeros((S, S), f32)
    for window, dil in ((128, 1), (512, 4), (2048, 16)):
        gap = np.abs(i[:, None] - i[None, :])
        times += (gap % dil == 0) & (gap // dil <= window // (2 * dil))
    off = lambda allowed: np.where(allowed, 0.0, NEG).astype(f32)

    def rope(rot, theta):
        inv = (f32(theta) ** (-np.arange(0, rot, 2, dtype=f32) / f32(rot))).astype(f32)
        ang = i.astype(f32)[:, None] * inv[None, :]
        cos, sin = (f(ang.astype(np.float64)).astype(f32) for f in (np.cos, np.sin))
        return np.stack([by_tile(np.concatenate([cos, cos], 1)), by_tile(np.concatenate([-sin, sin], 1))], 1)

    decay = np.zeros((P, 4, 384), f32)
    for h in range(4):
        log_g = np.log1p(-(2.0 ** (-5.0 - h)))
        dist = i[None, :] - i[:, None]
        full = np.where(dist >= 0, np.exp(log_g * np.maximum(dist, 0)), 0.0) * RD ** -0.5
        decay[:, h, :S] = full[:P]
        decay[:, h, S:] = full[P:, P:]
    return {
        "ident": np.eye(P, dtype=f32), "mask_a": by_tile(off(times > 0)), "mult_a": by_tile(times),
        "causal": by_tile(off(i[None, :] <= i[:, None])), "decay": decay,
        "rope_a": rope(32, 500000.0), "rope_b": rope(16, 500000.0), "rope_r": rope(RD, 10000.0),
    }


NAMES = ["x", "w_in", "lambda_qk", "w_out", "w_gate", "w_up", "w_down", "norm_final", "w_in_2", "w_ret_up_2",
         "w_moba_up_2", "w_out_2", "w_ffn_up_2", "w_ffn_down_2", "final_norm_w_2"]


def kernel(**inputs):
    from concourse import bacc
    from concourse.bass_utils import run_bass_kernel_spmd

    arrays = {n: np.ascontiguousarray(inputs[n]) for n in NAMES}
    arrays.update(tables())
    rows = [inputs[n].reshape(-1, P) for n in
            ("norm_attn", "norm_ffn", "attn_norm_w_2", "ffn_norm_w_2", "norm_final", "ret_norm_w_2", "subln")]
    arrays["gains"] = np.ascontiguousarray(np.concatenate(rows, 0).T)
    taps = np.concatenate([inputs["conv_w_2"][0], inputs["conv_b_2"]], 0)
    arrays["taps"] = np.ascontiguousarray(taps.reshape(4, -1, P).transpose(2, 0, 1))

    nc = bacc.Bacc("TRN2", target_bir_lowering=False, num_devices=1)
    ins = {n: nc.dram_tensor(f"in_{n}", a.shape, mybir.dt.from_np(a.dtype), kind="ExternalInput").ap()
           for n, a in arrays.items()}
    out = nc.dram_tensor("out", (1, S, D), F32, kind="ExternalOutput").ap()
    build(nc, ins, out)
    r = run_bass_kernel_spmd(nc, [{f"in_{n}": a for n, a in arrays.items()}], core_ids=[0])
    return r.results[0]["out"]
```
